# Optimizing a Trainium2 kernel written in Bass

```python
import math
import jax, jax.numpy as jnp
from jax import lax
import numpy as np

D_MODEL = 1024
BATCH = 1
SEQ = 256
DEPTH = 2

GRID_W = 64
CTX_LEN = 256
N_MIXERS = 2
POOL_WINDOWS = (2, 4, 8, 16)
POOL_GROUP = D_MODEL // len(POOL_WINDOWS)
DN_HEADS = 8
DN_DK = D_MODEL // DN_HEADS
DN_DV = D_MODEL // DN_HEADS
DN_CONV = 5
DN_CHUNK = 64
DN_HK = DN_HEADS * DN_DK
DN_HV = DN_HEADS * DN_DV
DN_PROJ = 2 * DN_HK + 2 * DN_HV + 4 * DN_HEADS
N_GROUPS = 4
EXPERTS_PER_GROUP = 4
N_EXPERTS = N_GROUPS * EXPERTS_PER_GROUP
TOP_K = 2
D_EXPERT = D_MODEL // 4
DEEPNORM_ALPHA = (2.0 * DEPTH) ** 0.25
DEEPNORM_BETA = (8.0 * DEPTH) ** -0.25
LN_EPS = 1e-5
N_POOL_LAYERS = (DEPTH + 1) // 2
N_DN_LAYERS = DEPTH // 2

kernel_name = "hybrid_pool_deltanet_moe_prefix_dit"

def layer_norm(x, g, b):
    xf = x.astype(jnp.float32)
    mu = jnp.mean(xf, -1, keepdims=True)
    var = jnp.mean(jnp.square(xf - mu), -1, keepdims=True)
    return ((xf - mu) * lax.rsqrt(var + LN_EPS) * g.astype(jnp.float32) + b.astype(jnp.float32)).astype(x.dtype)

def modulation(cvec, w_mod, b_mod):
    m = jax.nn.silu(cvec) @ w_mod + b_mod
    return jnp.split(m, 6, axis=-1)

def modulate(x, shift, scale):
    return x * (1 + scale) + shift

def post_norm(x, y, gate, g, b):
    return layer_norm(DEEPNORM_ALPHA * x + gate * y, g, b)

def box_mean(x, k, axis):
    n = x.shape[axis]
    cs = jnp.cumsum(x.astype(jnp.float32), axis=axis)
    zero = jnp.zeros_like(lax.slice_in_dim(cs, 0, 1, axis=axis))
    cs = jnp.concatenate([zero, cs], axis=axis)
    t = jnp.arange(n)
    lo = jnp.clip(t - k // 2, 0, n)
    hi = jnp.clip(t + k - k // 2, 0, n)
    s = jnp.take(cs, hi, axis=axis) - jnp.take(cs, lo, axis=axis)
    shape = [1] * x.ndim
    shape[axis] = n
    cnt = (hi - lo).astype(jnp.float32).reshape(shape)
    return (s / cnt).astype(x.dtype)

def pool_mixer(h, w_pool, scale, rows):
    B, L, D = h.shape
    outs = []
    for gi, k in enumerate(POOL_WINDOWS):
        hg = h[..., gi * POOL_GROUP:(gi + 1) * POOL_GROUP]
        if rows is None:
            m = box_mean(hg, k, 1)
        else:
            hg2 = hg.reshape(B, rows, GRID_W, POOL_GROUP)
            m = box_mean(box_mean(hg2, k, 1), k, 2).reshape(B, L, POOL_GROUP)
        outs.append(m - hg)
    p = jnp.stack(outs, axis=2)
    y = jnp.einsum('blgc,gcd->blgd', p, w_pool).reshape(B, L, D)
    return y * scale

def short_conv(u, w):
    K, C = w.shape
    pad = K // 2
    out = lax.conv_general_dilated(u, w.astype(u.dtype)[:, None, :], window_strides=(1,),
                                   padding=[(pad, K - 1 - pad)],
                                   dimension_numbers=('NWC', 'WIO', 'NWC'),
                                   feature_group_count=C)
    return jax.nn.silu(out)

def l2norm(t):
    return t * lax.rsqrt(jnp.sum(t * t, -1, keepdims=True) + 1e-6)

def gdn_chunked(q, k, v, g, beta, s0):
    B, H, L, dk = q.shape
    dv = v.shape[-1]
    C = DN_CHUNK
    N = L // C
    q = q.reshape(B, H, N, C, dk)
    k = k.reshape(B, H, N, C, dk)
    v = v.reshape(B, H, N, C, dv)
    g = jnp.cumsum(g.reshape(B, H, N, C), -1)
    beta = beta.reshape(B, H, N, C)
    tril = jnp.tril(jnp.ones((C, C), bool))
    strict = jnp.tril(jnp.ones((C, C), bool), -1)
    decay = jnp.exp(jnp.where(tril, g[..., :, None] - g[..., None, :], -jnp.inf))
    kb = k * beta[..., None]
    A = jnp.where(strict, jnp.einsum('bhnid,bhnjd->bhnij', kb, k) * decay, 0.0)
    eye = jnp.eye(C, dtype=A.dtype)
    rhs = jnp.concatenate([v * beta[..., None], kb * jnp.exp(g)[..., None]], -1)
    sol = lax.linalg.triangular_solve(eye + A, rhs, left_side=True, lower=True, unit_diagonal=True)
    u, w = sol[..., :dv], sol[..., dv:]
    qk = jnp.einsum('bhnid,bhnjd->bhnij', q, k) * decay
    q_dec = q * jnp.exp(g)[..., None]
    k_dec = k * jnp.exp(g[..., -1:] - g)[..., None]
    g_last = jnp.exp(g[..., -1])

    def step(S, xs):
        u_n, w_n, qk_n, qd_n, kd_n, gl_n = xs
        v_new = u_n - jnp.einsum('bhcd,bhde->bhce', w_n, S)
        o = jnp.einsum('bhcd,bhde->bhce', qd_n, S) + jnp.einsum('bhij,bhje->bhie', qk_n, v_new)
        S = S * gl_n[..., None, None] + jnp.einsum('bhcd,bhce->bhde', kd_n, v_new)
        return S, o

    xs = tuple(jnp.moveaxis(t, 2, 0) for t in (u, w, qk, q_dec, k_dec, g_last))
    S, o = lax.scan(step, s0, xs)
    o = jnp.moveaxis(o, 0, 2).reshape(B, H, L, dv)
    return o, S

def gdn_mixer(h, w_in, conv_w, a_log, dt_bias, norm_g, w_out, init_f, init_b):
    B, L, _ = h.shape
    f32 = jnp.float32
    proj = h @ w_in
    qkv = short_conv(proj[..., :2 * DN_HK + DN_HV], conv_w)
    z = proj[..., 2 * DN_HK + DN_HV:2 * DN_HK + 2 * DN_HV]
    o0 = 2 * DN_HK + 2 * DN_HV
    a = proj[..., o0:o0 + 2 * DN_HEADS].reshape(B, L, 2, DN_HEADS).astype(f32)
    b = proj[..., o0 + 2 * DN_HEADS:].reshape(B, L, 2, DN_HEADS).astype(f32)

    def heads(t, d):
        return t.reshape(B, L, DN_HEADS, d).transpose(0, 2, 1, 3).astype(f32)

    q = l2norm(heads(qkv[..., :DN_HK], DN_DK)) * (DN_DK ** -0.5)
    k = l2norm(heads(qkv[..., DN_HK:2 * DN_HK], DN_DK))
    v = heads(qkv[..., 2 * DN_HK:], DN_DV)
    g = -jnp.exp(a_log.astype(f32)) * jax.nn.softplus(a + dt_bias.astype(f32))
    g = g.transpose(2, 0, 3, 1)
    beta = jax.nn.sigmoid(b).transpose(2, 0, 3, 1)
    o_f, s_f = gdn_chunked(q, k, v, g[0], beta[0], init_f)
    rev = lambda t: jnp.flip(t, axis=2)
    o_b, s_b = gdn_chunked(rev(q), rev(k), rev(v), rev(g[1]), rev(beta[1]), init_b)
    o = o_f + rev(o_b)
    o = o * lax.rsqrt(jnp.mean(o * o, -1, keepdims=True) + 1e-6) * norm_g.astype(f32)
    o = o * jax.nn.silu(heads(z, DN_DV))
    o = o.transpose(0, 2, 1, 3).reshape(B, L, DN_HV).astype(h.dtype)
    return o @ w_out, s_f, s_b

def moe(h, w_router, b_router, w_gate, w_up, w_down):
    scores = jax.nn.sigmoid((h @ w_router).astype(jnp.float32))
    sel = scores + b_router.astype(jnp.float32)
    grp = sel.reshape(*sel.shape[:-1], N_GROUPS, EXPERTS_PER_GROUP)
    grp_score = jnp.sum(lax.top_k(grp, TOP_K)[0], -1)
    g_idx = jnp.argmax(grp_score, -1)
    in_group = jnp.take_along_axis(grp, g_idx[..., None, None], axis=-2)[..., 0, :]
    _, local = lax.top_k(in_group, TOP_K)
    e_idx = g_idx[..., None] * EXPERTS_PER_GROUP + local
    wts = jnp.take_along_axis(scores, e_idx, -1)
    wts = wts / jnp.sum(wts, -1, keepdims=True)
    combine = jnp.sum(jax.nn.one_hot(e_idx, N_EXPERTS, dtype=jnp.float32) * wts[..., None], -2)
    hid = jax.nn.silu(jnp.einsum('bld,edf->blef', h, w_gate)) * jnp.einsum('bld,edf->blef', h, w_up)
    y = jnp.einsum('blef,efd->bld', hid * combine[..., None].astype(hid.dtype), w_down)
    return y.astype(h.dtype)

def setup_inputs(seed: int = 0) -> dict:
    key = jax.random.key(seed)
    ks = jax.random.split(key, 20)
    D, E, F = D_MODEL, N_EXPERTS, D_EXPERT
    nrm = jax.random.normal
    x = nrm(ks[0], (BATCH, SEQ, D), jnp.float32)
    c = nrm(ks[1], (BATCH, D), jnp.float32)
    ctx = nrm(ks[2], (BATCH, CTX_LEN, D), jnp.float32)
    c_ctx = nrm(ks[3], (D,), jnp.float32)
    w_mod = nrm(ks[4], (DEPTH, D, 6 * D), jnp.float32) * D ** -0.5
    b_mod = 0.02 * nrm(ks[5], (DEPTH, 6 * D), jnp.float32)
    ln_g = 1.0 + 0.02 * nrm(ks[6], (DEPTH, 2, D), jnp.float32)
    ln_b = 0.02 * nrm(ks[7], (DEPTH, 2, D), jnp.float32)
    pool_w = nrm(ks[8], (N_POOL_LAYERS, len(POOL_WINDOWS), POOL_GROUP, POOL_GROUP), jnp.float32) * POOL_GROUP ** -0.5 * DEEPNORM_BETA
    pool_scale = 1.0 + 0.02 * nrm(ks[9], (N_POOL_LAYERS, D), jnp.float32)
    col_scale = jnp.ones((DN_PROJ,), jnp.float32).at[2 * DN_HK:2 * DN_HK + DN_HV].set(DEEPNORM_BETA)
    dn_w_in = nrm(ks[10], (N_DN_LAYERS, D, DN_PROJ), jnp.float32) * D ** -0.5 * col_scale
    dn_conv = nrm(ks[11], (N_DN_LAYERS, DN_CONV, 2 * DN_HK + DN_HV), jnp.float32) * DN_CONV ** -0.5
    dn_a_log = jnp.log(jax.random.uniform(ks[12], (N_DN_LAYERS, 2, DN_HEADS), jnp.float32, 1.0, 16.0))
    dt = jnp.exp(jax.random.uniform(ks[13], (N_DN_LAYERS, 2, DN_HEADS), jnp.float32, math.log(1e-3), math.log(1e-1)))
    dn_dt_bias = dt + jnp.log(-jnp.expm1(-dt))
    dn_norm = 1.0 + 0.02 * nrm(ks[14], (N_DN_LAYERS, DN_DV), jnp.float32)
    dn_w_out = nrm(ks[15], (N_DN_LAYERS, DN_HV, D), jnp.float32) * DN_HV ** -0.5 * DEEPNORM_BETA
    w_router = nrm(ks[16], (D, E), jnp.float32) * D ** -0.5
    b_router = 0.01 * nrm(ks[17], (E,), jnp.float32)
    kg, ku = jax.random.split(ks[18])
    w_gate = nrm(kg, (DEPTH, E, D, F), jnp.float32) * D ** -0.5
    w_up = nrm(ku, (DEPTH, E, D, F), jnp.float32) * D ** -0.5
    w_down = nrm(ks[19], (DEPTH, E, F, D), jnp.float32) * F ** -0.5 * DEEPNORM_BETA
    return {"x": x, "c": c, "ctx": ctx, "c_ctx": c_ctx, "w_mod": w_mod, "b_mod": b_mod,
            "ln_g": ln_g, "ln_b": ln_b, "pool_w": pool_w, "pool_scale": pool_scale,
            "dn_w_in": dn_w_in, "dn_conv": dn_conv, "dn_a_log": dn_a_log, "dn_dt_bias": dn_dt_bias,
            "dn_norm": dn_norm, "dn_w_out": dn_w_out, "w_router": w_router, "b_router": b_router,
            "w_gate": w_gate, "w_up": w_up, "w_down": w_down}

def reference(x, c, ctx, c_ctx, w_mod, b_mod, ln_g, ln_b, pool_w, pool_scale,
              dn_w_in, dn_conv, dn_a_log, dn_dt_bias, dn_norm, dn_w_out,
              w_router, b_router, w_gate, w_up, w_down):
    rows = x.shape[1] // GRID_W
    B = x.shape[0]
    for i in range(DEPTH):
        last = i == DEPTH - 1
        j = i // N_MIXERS
        ml = [t[:, None, :] for t in modulation(c, w_mod[i], b_mod[i])]
        mc = modulation(c_ctx, w_mod[i], b_mod[i])
        hx = modulate(x, ml[0], ml[1])
        hc = modulate(ctx, mc[0], mc[1])
        if i % N_MIXERS == 0:
            yx = pool_mixer(hx, pool_w[j], pool_scale[j], rows)
            yc = None if last else pool_mixer(hc, pool_w[j], pool_scale[j], None)
        else:
            zeros = jnp.zeros((B, DN_HEADS, DN_DK, DN_DV), jnp.float32)
            yc, s_f, s_b = gdn_mixer(hc, dn_w_in[j], dn_conv[j], dn_a_log[j], dn_dt_bias[j],
                                     dn_norm[j], dn_w_out[j], zeros, zeros)
            yx, _, _ = gdn_mixer(hx, dn_w_in[j], dn_conv[j], dn_a_log[j], dn_dt_bias[j],
                                 dn_norm[j], dn_w_out[j], s_f, s_b)
        x = post_norm(x, yx, ml[2], ln_g[i, 0], ln_b[i, 0])
        x = post_norm(x, moe(modulate(x, ml[3], ml[4]), w_router, b_router, w_gate[i], w_up[i], w_down[i]),
                      ml[5], ln_g[i, 1], ln_b[i, 1])
        if not last:
            ctx = post_norm(ctx, yc, mc[2], ln_g[i, 0], ln_b[i, 0])
            ctx = post_norm(ctx, moe(modulate(ctx, mc[3], mc[4]), w_router, b_router, w_gate[i], w_up[i], w_down[i]),
                            mc[5], ln_g[i, 1], ln_b[i, 1])
    return x


_drawn_inputs = setup_inputs


def setup_inputs(seed=0):
    import zlib

    import numpy as np

    out = dict(_drawn_inputs(seed))
    spreads = {}
    factors = {'ctx': 3.354, 'c_ctx': 2.984, 'pool_scale': 4.445, 'dn_norm': 11.103}
    for name, (base, spread) in spreads.items():
        noise = np.random.default_rng([zlib.crc32(name.encode()), seed]).standard_normal(out[name].shape)
        drawn = base * np.exp(spread * noise) if base else spread * noise
        out[name] = __import__('jax').numpy.asarray(drawn.astype(out[name].dtype))
    for name, factor in factors.items():
        out[name] = (out[name] * factor).astype(out[name].dtype)
    return out
```

```python
import math
from contextlib import ExitStack

import concourse.bass as bass
from concourse import mybir

F32 = mybir.dt.float32
I32 = mybir.dt.int32
ALU = mybir.AluOpType
ACT = mybir.ActivationFunctionType
AXX = mybir.AxisListType.X

P = 128
D = 1024
KD = D // P
SEQ = 256
CTX = 256
GRID_W = 64
DEPTH = 2
HALF = P // 2
MT = SEQ // HALF
XT = SEQ // P
N_GROUPS = 4
PER_GROUP = 4
N_EXPERTS = N_GROUPS * PER_GROUP
FE = D // 4
FC = FE // P
WINDOWS = (2, 4, 8, 16)
NW = len(WINDOWS)
PG = D // NW
HEADS = 8
TAPS = 5
ALPHA = (2.0 * DEPTH) ** 0.25
LN_EPS = 1e-5
L2_EPS = 1e-6
BANK = 512
NCH = 6 * D // BANK
SHIFT1, SCALE1, GATE1, SHIFT2, SCALE2, GATE2 = range(6)
CONV_ROWS = TAPS * 3 * D // P

C_IDENT, C_ONES, C_UPPER, C_UPPER_IN, C_LOWER_IN, C_IOTA = 0, 1, 2, 3, 4, 5
C_NEG_F, C_NEG_B = 9, 10
C_LEVEL_F, C_LEVEL_B = 11, 18
N_CONST = 25
LEVELS = 7


def declare(nc, ctx):
    class Names:
        pass
    m = Names()

    def sb(name, shape, dt=F32):
        return ctx.enter_context(nc.sbuf_tensor(name, shape, dt))

    m.const = sb("const", [P, N_CONST * P])
    m.x = sb("x_rows", [P, MT, D])
    m.h = sb("h_rows", [P, MT, D])
    m.hT = sb("h_cols", [P, KD, MT * P])
    m.mod = sb("modulation", [P, 6 * D])
    m.bias = sb("mod_bias", [P, 3, BANK])
    m.ln = sb("ln_vectors", [P, 2, D])
    m.ring = sb("weight_ring", [P, 6, 2048])
    m.arena = sb("arena", [P, 14336])
    m.c_rows = sb("c_rows", [2 * KD, P])
    m.c_silu = sb("c_silu", [2 * KD, P])
    m.small = sb("small", [P, 768])
    m.meta = sb("tile_counts", [P, 8], I32)
    m.ps = ctx.enter_context(nc.psum_tensor("banks", [P, 8, BANK], F32))
    return m


def columns(m):
    class Names:
        pass
    v = Names()
    c = m.const
    v.ident = c[:, C_IDENT * P:(C_IDENT + 1) * P]
    v.ones = c[:, C_ONES * P:(C_ONES + 1) * P]
    v.upper = c[:, C_UPPER * P:(C_UPPER + 1) * P]
    v.upper_in = c[:, C_UPPER_IN * P:(C_UPPER_IN + 1) * P]
    v.lower_in = c[:, C_LOWER_IN * P:(C_LOWER_IN + 1) * P]
    a = m.arena
    v.pool_m = a[:, 0:8192].rearrange("p (w t n) -> p w t n", w=NW, t=MT)
    v.pool_w = a[:, 8192:10240].rearrange("p (w c n) -> p w c n", w=NW, c=PG // P)
    v.tmp = a[:, 10240:12288].rearrange("p (b n) -> p b n", b=2)
    v.c_mix = a[:, 12288:13312].rearrange("p (k n) -> p k n", k=KD)
    v.c_lat = a[:, 13312:14336].rearrange("p (k n) -> p k n", k=KD)
    v.pool_scale = m.hT[:, 0:2, :].rearrange("p a n -> p (a n)")
    v.slots_T = a[:, 0:4096].rearrange("p (k n) -> p k n", k=KD)
    v.slots_y = a[:, 4096:8192].rearrange("p (s n) -> p s n", s=MT)
    v.onehot = a[:, 8192:8704].rearrange("p (t n) -> p t n", t=MT)
    v.onehot_T = a[:, 8704:9216]
    v.hidden = a[:, 9216:9472].rearrange("p (f n) -> p f n", f=FC)
    v.silu = a[:, 9472:9728].rearrange("p (f n) -> p f n", f=FC)
    v.slot_w = a[:, 9728:9792].rearrange("p (s e) -> p s e", s=MT)
    v.logits_T = a[0:N_EXPERTS, 8192:8704]
    v.y_rows = m.hT[:, :, :].rearrange("p k n -> p (k n)").rearrange("p (t n) -> p t n", t=MT)
    v.mod_ring = [m.ring[:, 2 * j:2 * j + 2, :].rearrange("p a (b n) -> p (a b) n", b=4) for j in range(3)]
    s = m.small
    v.w_router = s[:, 0:128].rearrange("p (k e) -> p k e", k=KD)
    v.b_router = s[:, 128:144]
    v.scores = s[:, 144:208]
    v.sel = s[:, 208:272]
    v.pairs = s[:, 272:368]
    v.combine = s[:, 368:432]
    v.better = s[:, 432:496]
    v.compare = s[:, 496:544]
    v.group_sum = s[:, 544:560]
    v.group_hot = s[:, 560:576]
    v.key = s[:, 576:592]
    v.totals = s[:, 592:608]
    v.group_max = s[:, 608:612]
    v.weight_sum = s[:, 612:616]
    v.desc = s[:, 616:620]
    v.counts = s[:, 620:624]
    v.tiles_f = s[:, 624:632]
    v.stats = s[:, 632:656].rearrange("p (b n) -> p b n", b=4)
    v.mean_var = s[:, 656:660].rearrange("p (b n) -> p b n", b=2)
    v.std = s[:, 660:662]
    v.rstd = s[:, 662:664]
    v.shift_ln = s[:, 664:666]
    return v


class Layer:

    def __init__(self, n, tiles, x_tiles):
        self.n, self.tiles, self.x_tiles = n, tiles, x_tiles
        self.tag = f"moe{n}_"
        self.h_base = n * MT


def build(nc, in_x, in_c, in_ctx, in_c_ctx, in_w_mod, in_b_mod,
          in_ln_g, in_ln_b, in_pool_w, in_pool_scale, in_dn_w_in, in_dn_conv,
          in_dn_a_log, in_dn_dt_bias, in_dn_norm, in_dn_w_out, in_w_router, in_b_router,
          in_w_gate, in_w_up, in_w_down,
          in_const, in_pool_m, out_dram):
    with ExitStack() as ctx:
        m = declare(nc, ctx)
        v = columns(m)
        sems = {}

        def s(name):
            if name not in sems:
                sems[name] = ctx.enter_context(nc.semaphore(name))
            return sems[name]

        L0 = Layer(0, MT, tuple(range(MT)))
        L1 = Layer(1, XT, (0, 2))
        LN_BASE = {"ln0a_": 0, "ln0b_": MT, "ln1a_": 2 * MT, "ln1b_": 2 * MT + XT}
        H_BASE = {"ln0a_": 0, "ln1a_": MT}
        block = ctx.enter_context(nc.Block())

        def mod_vec(which):
            return m.mod[:, which * D:(which + 1) * D]

        def sp_mod(sp, i, layer, first):
            for j in range(3):
                n = 3 * (i - 4 * layer) + j
                if not first:
                    sp.wait_ge(s("mod_mm"), 3 * i + j - 2)
                sp.dma_start(v.mod_ring[j],
                             in_w_mod[layer].rearrange("(k p) n -> p k n", p=P)[:, :, bass.ds(n * BANK, BANK)]
                             ).then_inc(s(f"mod_w{j}"), 16)
                if not first:
                    sp.wait_ge(s("mod_biased"), 3 * i + j - 2)
                sp.dma_start(m.bias[:, j, :],
                             in_b_mod[layer][bass.ds(n * BANK, BANK)].partition_broadcast(P)
                             ).then_inc(s(f"mod_b{j}"), 16)

        def pe_mod(pe, i, lhs, first):
            for j in range(3):
                pe.wait_ge(s(f"mod_w{j}"), 16 * i + 16)
                if not first:
                    pe.wait_ge(s("mod_copied"), 3 * i + j - 2)
                for k in range(KD):
                    mm = pe.matmul(m.ps[:, j, :], lhs(i, j)[:, k, :], v.mod_ring[j][:, k, :],
                                   start=(k == 0), stop=(k == KD - 1))
                mm.then_inc(s("mod_mm"), 1)

        def act_mod(act, i, layer):
            for j in range(3):
                n = 3 * (i - 4 * layer) + j
                act.wait_ge(s("mod_mm"), 3 * i + j + 1)
                act.copy(m.mod[:, bass.ds(n * BANK, BANK)], m.ps[:, j, :]).then_inc(s("mod_copied"), 1)

        def pool_mod(pool, i, layer):
            for j in range(3):
                n = 3 * (i - 4 * layer) + j
                pool.wait_ge(s("mod_copied"), 3 * i + j + 1)
                pool.wait_ge(s(f"mod_b{j}"), 16 * i + 16)
                dst = m.mod[:, bass.ds(n * BANK, BANK)]
                pool.tensor_tensor(dst, dst, m.bias[:, j, :], ALU.add).then_inc(s("mod_biased"), 1)

        def dve_norm(dve, tag, n, xt, y, y_wait, gate, mod_next, ln_wait):
            b = n % 2
            c = LN_BASE[tag] + n
            x = m.x[:, xt, :]
            tmp = v.tmp[:, b, :]
            y_wait(n)
            if n >= 2:
                dve.wait_ge(s("ln_gained"), c - 1)
            dve.tensor_tensor(tmp, y(n), gate, ALU.mult).then_inc(s("ln_gated"), 1)
            dve.wait_ge(s("ln_gated"), c + 1)
            dve.scalar_tensor_tensor(out=x, in0=x, scalar=ALPHA, in1=tmp, op0=ALU.mult,
                                     op1=ALU.add).then_inc(s("ln_summed"), 1)
            dve.wait_ge(s("ln_summed"), c + 1)
            for half in range(2):
                dve.bn_stats(v.stats[:, 2 * b + half, :], x[:, half * BANK:(half + 1) * BANK]).then_inc(s("ln_stats"), 1)
            dve.wait_ge(s("ln_stats"), 2 * c + 2)
            dve.bn_aggr(v.mean_var[:, b, :], v.stats[:, 2 * b:2 * b + 2, :]).then_inc(s("ln_var"), 1)
            dve.wait_ge(s("ln_std"), c + 1)
            dve.reciprocal(v.rstd[:, b:b + 1], v.std[:, b:b + 1]).then_inc(s("ln_rstd"), 1)
            dve.wait_ge(s("ln_rstd"), c + 1)
            dve.scalar_tensor_tensor(out=v.shift_ln[:, b:b + 1], in0=v.mean_var[:, b, 0:1], scalar=-1.0,
                                     in1=v.rstd[:, b:b + 1], op0=ALU.mult, op1=ALU.mult
                                     ).then_inc(s("ln_centre"), 1)
            ln_wait()
            dve.wait_ge(s("ln_normed"), c + 1)
            dve.tensor_tensor(tmp, tmp, m.ln[:, 0, :], ALU.mult).then_inc(s("ln_gained"), 1)
            dve.wait_ge(s("ln_gained"), c + 1)
            dve.tensor_tensor(x, tmp, m.ln[:, 1, :], ALU.add).then_inc(s("ln_x"), 1)
            if mod_next is not None:
                dve_modulate(dve, tag, n, xt, n, mod_next)

        def dve_modulate(dve, tag, n, xt, ht, which):
            c = LN_BASE[tag] + n
            dve.wait_ge(s("ln_x"), c + 1)
            h = m.h[:, ht, :]
            hc = H_BASE[tag] + n
            dve.scalar_tensor_tensor(out=h, in0=mod_vec(which[1]), scalar=1.0, in1=m.x[:, xt, :],
                                     op0=ALU.add, op1=ALU.mult).then_inc(s("ln_h_scaled"), 1)
            dve.wait_ge(s("ln_h_scaled"), hc + 1)
            dve.tensor_tensor(h, h, mod_vec(which[0]), ALU.add).then_inc(s("ln_h"), 1)

        def act_norm(act, tag, n, xt):
            b = n % 2
            c = LN_BASE[tag] + n
            act.wait_ge(s("ln_var"), c + 1)
            act.activation(v.std[:, b:b + 1], v.mean_var[:, b, 1:2], ACT.Sqrt, bias=v.eps).then_inc(s("ln_std"), 1)
            act.wait_ge(s("ln_centre"), c + 1)
            act.activation(v.tmp[:, b, :], m.x[:, xt, :], ACT.Identity, bias=v.shift_ln[:, b:b + 1],
                           scale=v.rstd[:, b:b + 1]).then_inc(s("ln_normed"), 1)

        v.eps = LN_EPS
        v.l2_eps = L2_EPS
        v.const_iota = m.const[:, C_IOTA * P:(C_IOTA + MT) * P]

        w_gate_flat = in_w_gate.rearrange("l e d f -> (l e d) f")
        w_up_flat = in_w_up.rearrange("l e d f -> (l e d) f")
        w_down_flat = in_w_down.rearrange("l e f d -> (l e f) d")

        def expert_dst(half):
            r = m.ring
            return (r[:, 3 * half, :].rearrange("p (k f) -> p k f", k=KD),
                    r[:, 3 * half + 1, :].rearrange("p (k f) -> p k f", k=KD),
                    r[:, 3 * half + 2, :].rearrange("p (k f) -> p k f", k=FC))

        def sp_expert(sp, L, e, half):
            srcs = (w_gate_flat, w_up_flat, w_down_flat)
            for w, dst in zip(srcs, expert_dst(half)):
                rows = D if w is not w_down_flat else FE
                base = (L.n * N_EXPERTS + e) * rows
                src = w[bass.ds(base, rows), :].rearrange("(k p) f -> p k f", p=P)
                sp.dma_start(dst, src).then_inc(s(L.tag + f"w{half}"), 16)

        def group_counts(eng, g):
            nt = eng.value_load(m.meta[0:1, bass.ds(g, 1)], min_val=1, max_val=MT)
            tb = eng.value_load(m.meta[0:1, bass.ds(g + N_GROUPS, 1)], min_val=0, max_val=MT * N_GROUPS)
            return nt, tb

        def sp_moe(sp, L):
            for e in range(2):
                sp_expert(sp, L, e, e)
            sp.wait_ge(s(L.tag + "meta"), 1)

            def group(g, more):
                nt, tb = group_counts(sp, g)
                for e in range(2 + 2 * more):
                    sp.wait_ge(s(L.tag + "down"), 4 * tb + (e + 1) * nt)
                    sp_expert(sp, L, 4 * g + e + 2, e % 2)
            with sp.Fori(0, N_GROUPS - 1) as g:
                group(g, True)
            group(N_GROUPS - 1, False)

        def sp_moe_drained(sp, L):
            nt, tb = group_counts(sp, N_GROUPS - 1)
            sp.wait_ge(s(L.tag + "down"), 4 * tb + 4 * nt)

        def pe_router(pe, L):
            t_ = L.tag
            for n in range(2 * L.tiles):
                t, half = divmod(n, 2)
                if half == 0:
                    pe.wait_ge(s("ln_h"), L.h_base + t + 1)
                if n >= 2:
                    pe.wait_ge(s(t_ + "hT"), n - 1)
                for k in range(4):
                    mm = pe.transpose(m.ps[:, 6 + n % 2, k * P:(k + 1) * P],
                                      m.h[:, t, (4 * half + k) * P:(4 * half + k + 1) * P], v.ident)
                mm.then_inc(s(t_ + "turned"), 1)
            pe.wait_ge(s(t_ + "hT"), 2 * L.tiles)
            pe.wait_ge(s("small_loads"), 32)
            for k in range(KD):
                mm = pe.matmul(m.ps[0:N_EXPERTS, 4, 0:L.tiles * P], v.w_router[:, k, :],
                               m.hT[:, k, 0:L.tiles * P], start=(k == 0), stop=(k == KD - 1))
            mm.then_inc(s(t_ + "logits"), 1)
            pe.wait_ge(s(t_ + "logits_T"), 1)
            for t in range(L.tiles):
                mm = pe.transpose(m.ps[:, 5, t * N_EXPERTS:(t + 1) * N_EXPERTS], v.logits_T[:, t * P:(t + 1) * P],
                                  v.ident[0:N_EXPERTS, 0:N_EXPERTS])
            mm.then_inc(s(t_ + "logit_rows"), 1)
            pe.wait_ge(s(t_ + "group_hot"), 1)
            w = L.tiles * N_GROUPS
            pe.matmul(m.ps[:, 4, 0:w], v.upper, v.group_hot[:, 0:w], start=True, stop=True)
            pe.matmul(m.ps[:, 4, 16:16 + w], v.ones, v.group_hot[:, 0:w], start=True, stop=True
                      ).then_inc(s(t_ + "ranks"), 1)

        def act_router(act, L):
            t_ = L.tag
            for n in range(2 * L.tiles):
                t, half = divmod(n, 2)
                act.wait_ge(s(t_ + "turned"), n + 1)
                act.copy(m.hT[:, 4 * half:4 * half + 4, t * P:(t + 1) * P],
                         m.ps[:, 6 + n % 2, :].rearrange("p (k n) -> p k n", k=4)).then_inc(s(t_ + "hT"), 1)
            act.wait_ge(s(t_ + "logits"), 1)
            act.copy(v.logits_T[:, 0:L.tiles * P], m.ps[0:N_EXPERTS, 4, 0:L.tiles * P]).then_inc(s(t_ + "logits_T"), 1)
            act.wait_ge(s(t_ + "logit_rows"), 1)
            act.activation(v.scores[:, 0:L.tiles * N_EXPERTS], m.ps[:, 5, 0:L.tiles * N_EXPERTS],
                           ACT.Sigmoid).then_inc(s(t_ + "scores"), 1)

        def dve_router(dve, L):
            t_ = L.tag
            T, E, G, Q = L.tiles, N_EXPERTS, N_GROUPS, PER_GROUP
            step = [0]

            def then(ins):
                step[0] += 1
                ins.then_inc(s(t_ + "route_step"), 1)
                dve.wait_ge(s(t_ + "route_step"), step[0])

            scores = v.scores[:, 0:T * E]
            sel = v.sel[:, 0:T * E]
            by_group = sel.rearrange("p (a q) -> p a q", q=Q)
            then(dve.tensor_scalar(v.desc, v.const_iota[:, 0:G], -1.0, G + 1.0, ALU.mult, ALU.add))
            dve.wait_ge(s("small_loads"), 32)
            dve.wait_ge(s(t_ + "scores"), 1)
            then(dve.tensor_tensor(sel.rearrange("p (t e) -> p t e", t=T), scores.rearrange("p (t e) -> p t e", t=T),
                                   v.b_router.unsqueeze(1).to_broadcast([P, T, E]), ALU.add))
            pairs = v.pairs[:, 0:T * G * 6].rearrange("p (a q) -> p a q", q=6)
            at = 0
            for d in range(1, Q):
                ins = dve.tensor_tensor(pairs[:, :, at:at + Q - d], by_group[:, :, 0:Q - d], by_group[:, :, d:Q], ALU.add)
                then(ins)
                at += Q - d
            gsum = v.group_sum[:, 0:T * G]
            gsum3 = gsum.rearrange("p (t g) -> p t g", t=T)
            ghot = v.group_hot[:, 0:T * G]
            ghot3 = ghot.rearrange("p (t g) -> p t g", t=T)
            gmax = v.group_max[:, 0:T]
            gmax3 = gmax.unsqueeze(2).to_broadcast([P, T, G])
            then(dve.tensor_reduce(gsum, pairs, AXX, ALU.max))
            then(dve.tensor_reduce(gmax, gsum3, AXX, ALU.max))
            then(dve.tensor_tensor(ghot3, gsum3, gmax3, ALU.is_equal))
            then(dve.tensor_tensor(gsum3, ghot3, v.desc.unsqueeze(1).to_broadcast([P, T, G]), ALU.mult))
            then(dve.tensor_reduce(gmax, gsum3, AXX, ALU.max))
            dve.tensor_tensor(ghot3, gsum3, gmax3, ALU.is_equal).then_inc(s(t_ + "group_hot"), 1)
            dve.wait_ge(s(t_ + "group_hot"), 1)
            better = v.better[:, 0:T * E].rearrange("p (a q) -> p a q", q=Q)
            cmp = v.compare[:, 0:T * G * 3].rearrange("p (a q) -> p a q", q=3)
            then(dve.tensor_scalar(better, v.desc.unsqueeze(1).to_broadcast([P, T * G, Q]), -1.0, None, ALU.add))
            for d in range(1, Q):
                then(dve.tensor_tensor(cmp[:, :, 0:Q - d], by_group[:, :, 0:Q - d], by_group[:, :, d:Q], ALU.is_ge))
                then(dve.tensor_tensor(better[:, :, d:Q], better[:, :, d:Q], cmp[:, :, 0:Q - d], ALU.add))
                then(dve.tensor_tensor(better[:, :, 0:Q - d], better[:, :, 0:Q - d], cmp[:, :, 0:Q - d], ALU.subtract))
            comb = v.combine[:, 0:T * E]
            then(dve.tensor_scalar(better, better, 2.0, None, ALU.is_lt))
            then(dve.tensor_tensor(better, better, ghot.unsqueeze(2).to_broadcast([P, T * G, Q]), ALU.mult))
            then(dve.tensor_tensor(comb, scores, v.better[:, 0:T * E], ALU.mult))
            wsum = v.weight_sum[:, 0:T]
            then(dve.tensor_reduce(wsum, comb.rearrange("p (t e) -> p t e", t=T), AXX, ALU.add))
            then(dve.reciprocal(wsum, wsum))
            then(dve.tensor_tensor(comb.rearrange("p (t e) -> p t e", t=T), comb.rearrange("p (t e) -> p t e", t=T),
                                   wsum.unsqueeze(2).to_broadcast([P, T, E]), ALU.mult))
            dve.wait_ge(s(t_ + "ranks"), 1)
            key = v.key[:, 0:T * G]
            tot = v.totals[:, 0:T * G]
            then(dve.tensor_scalar(key, m.ps[:, 4, 0:T * G], 1.0, None, ALU.add))
            then(dve.tensor_copy(tot, m.ps[:, 4, 16:16 + T * G]))
            for t in range(1, T):
                for u in range(t):
                    then(dve.tensor_tensor(key[:, t * G:(t + 1) * G], key[:, t * G:(t + 1) * G],
                                           tot[:, u * G:(u + 1) * G], ALU.add))
            then(dve.tensor_tensor(key, key, ghot, ALU.mult))
            then(dve.tensor_reduce(v.counts, tot.rearrange("p (t g) -> p g t", t=T), AXX, ALU.add))
            tiles, before = v.tiles_f[:, 0:G], v.tiles_f[:, G:2 * G]
            then(dve.tensor_scalar(tiles, v.counts, float(P), 1.0, ALU.is_gt, ALU.add))
            for t in range(2, T):
                then(dve.scalar_tensor_tensor(out=tiles, in0=v.counts, scalar=float(t * P), in1=tiles,
                                              op0=ALU.is_gt, op1=ALU.add))
            then(dve.memset(before, 0.0))
            for g in range(1, G):
                then(dve.tensor_tensor(before[:, g:g + 1], before[:, g - 1:g], tiles[:, g - 1:g], ALU.add))
            dve.tensor_copy(m.meta[:, :], v.tiles_f).then_inc(s(t_ + "meta"), 1)
            dve.wait_ge(s(t_ + "meta"), 1)
            dve.memset(v.y_rows[:, 0:T, :], 0.0).then_inc(s(t_ + "y_added"), 1)

        def pe_moe(pe, L):
            t_ = L.tag
            T = L.tiles
            pe.wait_ge(s(t_ + "meta"), 1)
            with pe.Fori(0, N_GROUPS) as g:
                nt, tb = group_counts(pe, g)
                with pe.Fori(0, nt) as i:
                    q = tb + i
                    pe.wait_ge(s(t_ + "onehot"), q + 1)
                    pe.wait_ge(s(t_ + "slots_T_free"), 2 * q + 2)
                    for half in range(2):
                        for k in range(4):
                            for t in range(T):
                                mm = pe.matmul(m.ps[:, 6 + half, k * P:(k + 1) * P],
                                               m.h[:, t, (4 * half + k) * P:(4 * half + k + 1) * P],
                                               v.onehot[:, t, :], start=(t == 0), stop=(t == T - 1))
                        mm.then_inc(s(t_ + "gathered"), 1)
                    pe.wait_ge(s(t_ + "slot_w"), q + 1)
                    for t in range(T):
                        mm = pe.matmul(m.ps[:, 4, 0:N_EXPERTS], v.onehot[:, t, :],
                                       v.combine[:, t * N_EXPERTS:(t + 1) * N_EXPERTS],
                                       start=(t == 0), stop=(t == T - 1))
                    mm.then_inc(s(t_ + "weights_gathered"), 1)
                for e in range(PER_GROUP):
                    half = e % 2
                    wg, wu, wd = expert_dst(half)
                    with pe.Fori(0, nt) as i:
                        if e == 0:
                            pe.wait_ge(s(t_ + "slots_T_free"), 2 * tb + 2 * nt + 2)
                        pe.wait_ge(s(t_ + f"w{half}"), 96 * g + 48 * (e // 2) + 48)
                        q = 4 * tb + e * nt + i
                        for f in range(FC):
                            pe.wait_ge(s(t_ + "hidden"), 2 * q + f + 1)
                            for w, c in ((wg, 0), (wu, 1)):
                                for k in range(KD):
                                    mm = pe.matmul(m.ps[:, f, c * P:(c + 1) * P], w[:, k, f * P:(f + 1) * P],
                                                   v.slots_T[:, k, bass.ds(i * P, P)],
                                                   start=(k == 0), stop=(k == KD - 1))
                            mm.then_inc(s(t_ + "gate_up"), 1)
                        pe.wait_ge(s(t_ + "summed"), q + 1)
                        for f in range(FC):
                            pe.wait_ge(s(t_ + "hidden"), 2 * q + f + 3)
                            for half_d in range(2):
                                mm = pe.matmul(m.ps[:, 2 + half_d, :], v.hidden[:, f, :],
                                               wd[:, f, half_d * BANK:(half_d + 1) * BANK],
                                               start=(f == 0), stop=(f == FC - 1))
                        mm.then_inc(s(t_ + "down"), 1)
                with pe.Fori(0, nt) as i:
                    q = tb + i
                    pe.wait_ge(s(t_ + "onehot_again"), q + 1)
                    pe.wait_ge(s(t_ + "onehot_T"), q + 1)
                    for t in range(T):
                        mm = pe.transpose(m.ps[:, 5, t * P:(t + 1) * P], v.onehot[:, t, :], v.ident)
                    mm.then_inc(s(t_ + "onehot_turned"), 1)
                    pe.wait_ge(s(t_ + "onehot_T"), q + 2)
                    pe.wait_ge(s(t_ + "summed"), 4 * tb + 4 * nt + 1)
                    for n in range(2 * T):
                        t, half = divmod(n, 2)
                        pe.wait_ge(s(t_ + "y_added"), 2 * T * q + n + 1)
                        pe.matmul(m.ps[:, 6 + half, :], v.onehot_T[:, t * P:(t + 1) * P],
                                  v.slots_y[:, i, half * BANK:(half + 1) * BANK], start=True, stop=True
                                  ).then_inc(s(t_ + "spread"), 1)

        def act_moe(act, L):
            t_ = L.tag
            T = L.tiles
            act.wait_ge(s(t_ + "meta"), 1)
            act.sem_inc(s(t_ + "slots_T_free"), 2)
            act.sem_inc(s(t_ + "onehot_T"), 1)
            with act.Fori(0, N_GROUPS) as g:
                nt, tb = group_counts(act, g)
                with act.Fori(0, nt) as i:
                    q = tb + i
                    for half in range(2):
                        act.wait_ge(s(t_ + "gathered"), 2 * q + half + 1)
                        act.copy(v.slots_T[:, 4 * half:4 * half + 4, bass.ds(i * P, P)],
                                 m.ps[:, 6 + half, :].rearrange("p (k n) -> p k n", k=4)
                                 ).then_inc(s(t_ + "slots_T_free"), 1)
                for e in range(PER_GROUP):
                    with act.Fori(0, nt) as i:
                        q = 4 * tb + e * nt + i
                        for f in range(FC):
                            act.wait_ge(s(t_ + "gate_up"), 2 * q + f + 1)
                            act.activation(v.silu[:, f, :], m.ps[:, f, 0:P], ACT.Silu).then_inc(s(t_ + "silu"), 1)
                with act.Fori(0, nt) as i:
                    q = tb + i
                    act.wait_ge(s(t_ + "onehot_turned"), q + 1)
                    act.copy(v.onehot_T[:, 0:T * P], m.ps[:, 5, 0:T * P]).then_inc(s(t_ + "onehot_T"), 1)

        def dve_moe(dve, L):
            t_ = L.tag
            T = L.tiles
            dve.sem_inc(s(t_ + "y_added"), 1)
            dve.sem_inc(s(t_ + "slot_w"), 1)
            dve.sem_inc(s(t_ + "hidden"), 2)
            dve.sem_inc(s(t_ + "summed"), 1)

            def onehots(g, i, sem):
                for t in range(T):
                    ins = dve.tensor_scalar(v.onehot[:, t, :], v.const_iota[:, bass.ds(i * P, P)],
                                            v.key[:, bass.ds(g + t * N_GROUPS, 1)], None, ALU.is_equal)
                ins.then_inc(s(sem), 1)

            with dve.Fori(0, N_GROUPS) as g:
                nt, tb = group_counts(dve, g)
                with dve.Fori(0, nt) as i:
                    q = tb + i
                    onehots(g, i, t_ + "onehot")
                    dve.wait_ge(s(t_ + "weights_gathered"), q + 1)
                    dve.tensor_copy(v.slot_w[:, i, :], m.ps[:, 4, 0:N_EXPERTS]).then_inc(s(t_ + "slot_w"), 1)
                for e in range(PER_GROUP):
                    with dve.Fori(0, nt) as i:
                        q = 4 * tb + e * nt + i
                        for f in range(FC):
                            dve.wait_ge(s(t_ + "silu"), 2 * q + f + 1)
                            dve.tensor_tensor(v.hidden[:, f, :], v.silu[:, f, :], m.ps[:, f, P:2 * P], ALU.mult
                                              ).then_inc(s(t_ + "hidden"), 1)
                        dve.wait_ge(s(t_ + "down"), q + 1)
                        dve.wait_ge(s(t_ + "summed"), q + 1)
                        down = m.ps[:, 2:4, :].rearrange("p a n -> p (a n)")
                        w = v.slot_w[:, i, bass.ds(PER_GROUP * g + e, 1)]
                        y = v.slots_y[:, i, :]
                        if e == 0:
                            dve.wait_ge(s(t_ + "slot_w"), tb + nt + 1)
                            ins = dve.tensor_scalar(y, down, w, None, ALU.mult)
                        else:
                            ins = dve.scalar_tensor_tensor(out=y, in0=down, scalar=w, in1=y, op0=ALU.mult, op1=ALU.add)
                        ins.then_inc(s(t_ + "summed"), 1)
                with dve.Fori(0, nt) as i:
                    q = tb + i
                    onehots(g, i, t_ + "onehot_again")
                    for n in range(2 * T):
                        t, half = divmod(n, 2)
                        dve.wait_ge(s(t_ + "spread"), 2 * T * q + n + 1)
                        dst = v.y_rows[:, t, half * BANK:(half + 1) * BANK]
                        dve.wait_ge(s(t_ + "y_added"), 2 * T * q + n + 2)
                        dve.tensor_tensor(dst, dst, m.ps[:, 6 + half, :], ALU.add).then_inc(s(t_ + "y_added"), 1)

        def pe_pool(pe):
            for c in range(KD):
                if c == 0:
                    pe.wait_ge(s("in0_h"), MT)
                    pe.wait_ge(s("pool_m"), 16)
                if c >= 2:
                    pe.wait_ge(s("pooled_T"), c - 1)
                for t in range(MT):
                    mm = pe.matmul(m.ps[:, 3 + c % 2, :], m.h[:, t, c * P:(c + 1) * P], v.pool_m[:, c * P // PG, t, :],
                                   start=(t == 0), stop=(t == MT - 1))
                mm.then_inc(s("pooled"), 1)
            pe.wait_ge(s("pooled_T"), KD)
            pe.wait_ge(s("pool_w"), 16)
            for t in range(MT):
                if t >= 2:
                    pe.wait_ge(s("ln_gated"), t - 1)
                flat = m.ps[:, 3 + 2 * (t % 2):5 + 2 * (t % 2), :].rearrange("p a n -> p (a n)")
                for w in range(NW):
                    for c in range(PG // P):
                        mm = pe.matmul(flat[:, w * PG:(w + 1) * PG], m.hT[:, 2 * w + c, t * P:(t + 1) * P],
                                       v.pool_w[:, w, c, :], start=(c == 0), stop=(c == PG // P - 1))
                mm.then_inc(s("pool_y"), 1)

        def act_pool(act):
            act.wait_ge(s("pool_gate"), 1)
            for c in range(KD):
                act.wait_ge(s("pooled"), c + 1)
                act.copy(m.hT[:, c, :], m.ps[:, 3 + c % 2, :]).then_inc(s("pooled_T"), 1)

        def pool_y(t):
            return m.ps[:, 3 + 2 * (t % 2):5 + 2 * (t % 2), :].rearrange("p a n -> p (a n)")

        TT = (CTX + SEQ) // P
        CT = CTX // P
        ORDER = ((0, 1, 2, 3), (1, 0, 3, 2))
        a = m.arena
        at = [0]

        def take(n, shape=None, **kw):
            r = a[:, at[0]:at[0] + n]
            at[0] += n
            return r.rearrange(shape, **kw) if shape else r
        pad = [take(2 * 260, "p (s n) -> p s n", s=2), take(2 * 260, "p (s n) -> p s n", s=2),
               take(260, "p (s n) -> p s n", s=1)]
        conv = [take(512), take(512), take(256)]
        k_rows = take(512, "p (t n) -> p t n", t=TT)
        v_rows = take(512, "p (t n) -> p t n", t=TT)
        q_rows = take(256, "p (t n) -> p t n", t=XT)
        square = take(512, "p (t n) -> p t n", t=TT)
        square_q = take(256, "p (t n) -> p t n", t=XT)
        kT = take(512)
        qT = take(256)
        exp_q = [square[:, XT * d:XT * d + XT, :].rearrange("p t n -> p (t n)") for d in range(2)]
        qT_dec = [take(256) for _ in range(2)]
        decay = [take(512, "p (t n) -> p t n", t=TT) for _ in range(2)]
        NBT = [take(512, "p (t n) -> p t n", t=TT) for _ in range(2)]
        QK = [take(256, "p (t n) -> p t n", t=XT) for _ in range(2)]
        X = [take(512, "p (t n) -> p t n", t=TT) for _ in range(2)]
        XTr = [take(512, "p (t n) -> p t n", t=TT) for _ in range(2)]
        Pm = [take(512, "p (t n) -> p t n", t=TT) for _ in range(2)]
        diag = Pm
        state = [take(128) for _ in range(2)]
        rest = [take(128) for _ in range(2)]
        v_new = [take(128) for _ in range(2)]
        v_dec = rest
        z_silu = take(256, "p (t n) -> p t n", t=XT)
        z_gate = take(256, "p (t n) -> p t n", t=XT)
        o_rows = take(256, "p (t n) -> p t n", t=XT)
        norm_g = take(128)
        taps = take(128)
        w_ab = take(256, "p (k n) -> p k n", k=KD)
        NV = 2 * HEADS
        gc, neg_eg, beta, bdec, g_last, gate_a, total, soft = [take(64) for _ in range(8)]
        dt_b, a_neg = take(16), take(16)
        norms, rnorm = take(6), take(6)
        o_ss, o_rs = take(2), take(2)
        assert at[0] <= 14336, at[0]
        conv_rows = k_rows.rearrange("p t n -> p (t n)")[0:CONV_ROWS, 0:P]
        abT = square.rearrange("p t n -> p (t n)")[0:2 * NV, :]
        oT = m.mod[:, 0:HEADS * SEQ].rearrange("p (h n) -> p h n", h=HEADS)
        head_w = [m.ring[:, 2 * b:2 * b + 2, :].rearrange("p a (c k n) -> p (a c) k n", c=2, k=KD) for b in range(2)]
        w_out = [m.h[:, :, :], m.ring[:, 4:6, :].rearrange("p a (c n) -> p (a c) n", c=2)]

        def vec(x, t, d, h):
            return x[:, bass.ds(t * NV + d * HEADS + h, 1)]

        def vecs(x, d, h):
            return x.rearrange("p (t c) -> p t c", t=TT)[:, :, bass.ds(d * HEADS + h, 1)].to_broadcast([P, TT, P])

        def marks(keys):
            return {k: n + 1 for n, k in enumerate(keys)}
        DIRS = (0, 1)
        LAST = LEVELS - 1
        XP = marks([(n, d, k) for n in range(1, LEVELS) for d in DIRS for k in ("XP", "XPT") if n < LAST or k == "XPT"])
        XD = marks([(n, d, k) for n in range(LEVELS) for d in DIRS for k in ("X", "XT") if n < LAST or k == "XT"])
        RP = marks([(k, st, d) for st in range(TT) for k in ("kS", "v", "S") for d in DIRS
                    if not (k == "kS" and st == 0) and not (k == "S" and st == TT - 1)])
        RD = marks([(k, st, d) for st in range(TT) for ks in (("r",), ("vd", "vn"), ("S",)) for d in DIRS for k in ks
                    if not (k == "r" and st == 0) and not (k in ("vd", "S") and st == TT - 1)
                    and not (k == "vn" and st < CT)])

        def bank(n):
            return m.ps[:, n, :]

        def bank4(n):
            return m.ps[:, n, :].rearrange("p (t n) -> p t n", t=TT)

        def P_bank(d):
            return 3 * d

        def sp_heads_first(sp):
            sp.dma_start(conv_rows, in_dn_conv[0].rearrange("j (c n) -> (j c) n", n=P)).then_inc(s("dn_small"), 16)
            sp.dma_start(w_ab, in_dn_w_in[0].rearrange("(k p) n -> p k n", p=P)[:, :, 4 * D:4 * D + 2 * NV]
                         ).then_inc(s("dn_small"), 16)
            sp.dma_start(dt_b, in_dn_dt_bias[0].rearrange("d h -> (d h)").partition_broadcast(P)).then_inc(s("dn_small"), 16)
            sp.dma_start(a_neg, in_dn_a_log[0].rearrange("d h -> (d h)").partition_broadcast(P)).then_inc(s("dn_small"), 16)
            sp.dma_start(norm_g, in_dn_norm[0].partition_broadcast(P)).then_inc(s("dn_small"), 16)

        def sp_head(sp, h, b):
            w = in_dn_w_in[0].rearrange("(k p) n -> p k n", p=P)
            for j, c in enumerate((1, 2, 0, 3)):
                sp.dma_start(head_w[b][:, j, :, :], w[:, :, bass.ds(c * D + h * P, P)]).then_inc(s(f"head_w{b}"), 16)

        def pe_project(pe, h, b, j):
            if j == 0:
                pe.wait_ge(s(f"head_w{b}"), 64 * ((h - b) // 2) + 64 if isinstance(h, int) else 32 * (h - b) + 64)
            if not (isinstance(h, int) and 4 * h + j < 2):
                pe.wait_ge(s("proj_read"), 4 * h + j - 1)
            w = head_w[b][:, j, :, :]
            if j < 3:
                n0 = 0 if j < 2 else CTX
                for k in range(KD):
                    mm = pe.matmul(bank(6 + j % 2)[:, 0:CTX + SEQ - n0], w[:, k, :], m.hT[:, k, n0:CTX + SEQ],
                                   start=(k == 0), stop=(k == KD - 1))
            else:
                for t in range(XT):
                    for k in range(KD):
                        mm = pe.matmul(bank(7)[:, t * P:(t + 1) * P], m.hT[:, k, CTX + t * P:CTX + (t + 1) * P],
                                       w[:, k, :], start=(k == 0), stop=(k == KD - 1))
            mm.then_inc(s("projected"), 1)

        def act_project(act, h, j):
            act.wait_ge(s("projected"), 4 * h + j + 1)
            zero = isinstance(h, int) and h == 0
            if j < 3:
                if not zero:
                    act.wait_ge(s("conv_step"), 3 * TAPS * (h - 1) + TAPS * (j + 1))
                n = 2 if j < 2 else 1
                act.copy(pad[j][:, :, 2:2 + SEQ], bank(6 + j % 2)[:, 0:n * SEQ].rearrange("p (s n) -> p s n", s=n)
                         ).then_inc(s("proj_read"), 1)
            else:
                if not zero:
                    act.wait_ge(s("z_gate"), h)
                act.activation(z_silu, bank(7)[:, 0:SEQ].rearrange("p (t n) -> p t n", t=XT), ACT.Silu
                               ).then_inc(s("proj_read"), 1)

        def dve_conv(dve, h, j):
            dve.wait_ge(s("proj_read"), 4 * h + j + 1)
            n = 2 if j < 2 else 1
            out = conv[j].rearrange("p (s n) -> p s n", s=n)
            chunk = (HEADS, 2 * HEADS, 0)[j]
            for c in range(TAPS):
                tap = taps[:, bass.ds(c * 3 * HEADS + chunk + h, 1)]
                src = pad[j][:, :, c:c + SEQ]
                if c == 0:
                    ins = dve.tensor_scalar(out, src, tap, None, ALU.mult)
                else:
                    dve.wait_ge(s("conv_step"), 3 * TAPS * h + TAPS * j + c)
                    ins = dve.scalar_tensor_tensor(out=out, in0=src, scalar=tap, in1=out, op0=ALU.mult, op1=ALU.add)
                ins.then_inc(s("conv_step"), 1)

        def act_conv(act, h, j):
            act.wait_ge(s("conv_step"), 3 * TAPS * h + TAPS * (j + 1))
            act.activation(conv[j], conv[j], ACT.Silu).then_inc(s("conv_silu"), 1)

        def pe_prepare(pe, h):
            for j, n in ((0, TT), (1, TT), (2, XT)):
                pe.wait_ge(s("conv_silu"), 3 * h + j + 1)
                for t in range(n):
                    mm = pe.transpose(bank(j)[:, t * P:(t + 1) * P], conv[j][:, t * P:(t + 1) * P], v.ident)
                mm.then_inc(s("rows_turned"), 1)
            for d in DIRS:
                pe.wait_ge(s("diag"), 2 * h + d + 1)
                pe.wait_ge(s("rows"), 3 * h + d + 1)
                pe.matmul(bank(d), v.ones, diag[d].rearrange("p t n -> p (t n)"), start=True, stop=True
                          ).then_inc(s("along"), 1)
            pe.wait_ge(s("k_normed"), h + 1)
            for t in range(TT):
                mm = pe.transpose(bank(3)[:, t * P:(t + 1) * P], k_rows[:, t, :], v.ident)
            mm.then_inc(s("normed_turned"), 1)
            pe.wait_ge(s("q_normed"), h + 1)
            for t in range(XT):
                mm = pe.transpose(bank(2)[:, t * P:(t + 1) * P], q_rows[:, t, :], v.ident)
            mm.then_inc(s("normed_turned"), 1)
            pe.wait_ge(s("normed_T"), 2 * h + 2)
            for t in range(TT):
                pe.matmul(bank(4)[:, t * P:(t + 1) * P], kT[:, t * P:(t + 1) * P], kT[:, t * P:(t + 1) * P],
                          start=True, stop=True)
            for t in range(XT):
                mm = pe.matmul(bank(5)[:, t * P:(t + 1) * P], kT[:, (CT + t) * P:(CT + t + 1) * P],
                               qT[:, t * P:(t + 1) * P], start=True, stop=True)
            mm.then_inc(s("products"), 1)

        def pool_head(pool, h, first):
            if not first:
                pool.wait_ge(s("inv_xp"), len(XP) * h)
            for d in DIRS:
                pool.tensor_tensor(diag[d], v.ident.unsqueeze(1).to_broadcast([P, TT, P]), vecs(gc, d, h), ALU.mult
                                   ).then_inc(s("diag"), 1)

        def pool_gate(pool, h, first):
            pool.wait_ge(s("proj_read"), 4 * h + 4)
            if not first:
                pool.wait_ge(s("o_gated"), h)
            pool.tensor_tensor(z_gate, z_silu, norm_g.unsqueeze(1).to_broadcast([P, XT, P]), ALU.mult
                               ).then_inc(s("z_gate"), 1)

        def act_prepare_rows(act, h):
            for j, dst in ((0, k_rows), (1, v_rows), (2, q_rows)):
                act.wait_ge(s("rows_turned"), 3 * h + j + 1)
                n = TT if j < 2 else XT
                act.copy(dst, bank(j)[:, 0:n * P].rearrange("p (t n) -> p t n", t=n)).then_inc(s("rows"), 1)

        def act_prepare(act, h):
            act.wait_ge(s("squares"), h + 1)
            act.activation(norms, norms, ACT.Sqrt, bias=v.l2_eps).then_inc(s("norms"), 1)
            act.wait_ge(s("normed_turned"), 2 * h + 1)
            act.copy(kT, bank(3)).then_inc(s("normed_T"), 1)
            act.wait_ge(s("normed_turned"), 2 * h + 2)
            act.copy(qT, bank(2)[:, 0:SEQ]).then_inc(s("normed_T"), 1)
            for d in DIRS:
                act.wait_ge(s("decay_exp"), 2 * h + d + 1)
                act.activation(exp_q[d], bank(d)[:, CTX:CTX + SEQ], ACT.Exp).then_inc(s("exp_q"), 1)
                act.activation(decay[d], decay[d], ACT.Exp).then_inc(s("decay"), 1)

        PREP = 13

        def dve_prepare(dve, h):
            n = [0]

            def then(ins):
                n[0] += 1
                ins.then_inc(s("prep_step"), 1)
                dve.wait_ge(s("prep_step"), PREP * h + n[0])
            dve.wait_ge(s("rows"), 3 * h + 1)
            then(dve.tensor_tensor(square, k_rows, k_rows, ALU.mult))
            then(dve.tensor_reduce(norms[:, 0:TT], square, AXX, ALU.add))
            dve.wait_ge(s("rows"), 3 * h + 3)
            then(dve.tensor_tensor(square_q, q_rows, q_rows, ALU.mult))
            dve.tensor_reduce(norms[:, TT:TT + XT], square_q, AXX, ALU.add).then_inc(s("squares"), 1)
            for d in DIRS:
                neg = m.const[:, (C_NEG_F + d) * P:(C_NEG_F + d + 1) * P].unsqueeze(1).to_broadcast([P, TT, P])
                dve.wait_ge(s("along"), 2 * h + d + 1)
                then(dve.tensor_tensor(decay[d], bank4(d), neg, ALU.add))
                dve.tensor_tensor(decay[d], decay[d], vecs(gc, d, h), ALU.subtract).then_inc(s("decay_exp"), 1)
            dve.wait_ge(s("norms"), h + 1)
            then(dve.reciprocal(rnorm, norms))
            then(dve.tensor_scalar(rnorm[:, TT:TT + XT], rnorm[:, TT:TT + XT], float(P) ** -0.5, None, ALU.mult))
            dve.tensor_tensor(k_rows, k_rows, rnorm[:, 0:TT].unsqueeze(2).to_broadcast([P, TT, P]), ALU.mult
                              ).then_inc(s("k_normed"), 1)
            dve.tensor_tensor(q_rows, q_rows, rnorm[:, TT:TT + XT].unsqueeze(2).to_broadcast([P, XT, P]), ALU.mult
                              ).then_inc(s("q_normed"), 1)
            dve.wait_ge(s("products"), h + 1)
            for d in DIRS:
                dve.wait_ge(s("decay"), 2 * h + d + 1)
                then(dve.tensor_tensor(NBT[d], decay[d], bank4(4), ALU.mult))
                dve.tensor_tensor(NBT[d], NBT[d], vecs(beta, d, h), ALU.mult).then_inc(s("nbt"), 1)
                then(dve.tensor_tensor(QK[d], decay[d][:, CT:TT, :],
                                       bank(5)[:, 0:SEQ].rearrange("p (t n) -> p t n", t=XT), ALU.mult))
                then(dve.tensor_tensor(qT_dec[d], qT, exp_q[d], ALU.mult))

        def pe_inverse(pe, h, filler):
            for n in range(LEVELS):
                for d in DIRS:
                    if n == 0:
                        pe.wait_ge(s("nbt"), 2 * h + d + 1)
                        pe.wait_ge(s("prep_step"), PREP * h + PREP)
                    else:
                        pe.wait_ge(s("inv_x"), len(XD) * h + XD[n - 1, d, "X"])
                    for t in range(TT):
                        mm = pe.matmul(bank(P_bank(d))[:, t * P:(t + 1) * P], NBT[d][:, t, :],
                                       v.ident if n == 0 else X[d][:, t, :], start=True, stop=True)
                    mm.then_inc(s("inv_p"), 1)
                filler(n)
                if n == 0:
                    continue
                for d in DIRS:
                    pe.wait_ge(s("inv_pm"), 2 * LEVELS * h + 2 * n + d + 1)
                    pe.wait_ge(s("inv_x"), len(XD) * h + XD[n - 1, d, "XT"])
                    for kind in ("XP", "XPT"):
                        if (n, d, kind) not in XP:
                            continue
                        for t in range(TT):
                            l, r = (XTr[d], Pm[d]) if kind == "XP" else (Pm[d], XTr[d])
                            mm = pe.matmul(bank(P_bank(d) + (1 if kind == "XP" else 2))[:, t * P:(t + 1) * P],
                                           l[:, t, :], r[:, t, :], start=True, stop=True)
                        mm.then_inc(s("inv_xp"), 1)

        def dve_inverse(dve, h, filler):
            for n in range(LEVELS):
                for d in DIRS:
                    level = m.const[:, ((C_LEVEL_F, C_LEVEL_B)[d] + n) * P:((C_LEVEL_F, C_LEVEL_B)[d] + n + 1) * P]
                    dve.wait_ge(s("inv_p"), 2 * LEVELS * h + 2 * n + d + 1)
                    dve.tensor_tensor(Pm[d], bank4(P_bank(d)), level.unsqueeze(1).to_broadcast([P, TT, P]), ALU.mult
                                      ).then_inc(s("inv_pm"), 1)
                if n == 0:
                    for d in DIRS:
                        turned = (C_LEVEL_B, C_LEVEL_F)[d]
                        level = m.const[:, turned * P:(turned + 1) * P].unsqueeze(1).to_broadcast([P, TT, P])
                        eye = v.ident.unsqueeze(1).to_broadcast([P, TT, P])
                        dve.wait_ge(s("inv_pm"), 2 * LEVELS * h + d + 1)
                        dve.tensor_tensor(X[d], eye, Pm[d], ALU.subtract).then_inc(s("inv_x"), 1)
                        dve.tensor_tensor(decay[d], NBT[d], level, ALU.mult).then_inc(s("first_masked"), 1)
                        dve.wait_ge(s("first_masked"), 2 * h + d + 1)
                        dve.tensor_tensor(XTr[d], eye, decay[d], ALU.subtract).then_inc(s("inv_x"), 1)
                else:
                    for d in DIRS:
                        for kind, dst, b in (("X", X[d], 1), ("XT", XTr[d], 2)):
                            if (n, d, kind) not in XD:
                                continue
                            dve.wait_ge(s("inv_xp"), len(XP) * h + XP[n, d, "XP" if kind == "X" else "XPT"])
                            dve.tensor_tensor(dst, dst, bank4(P_bank(d) + b), ALU.subtract).then_inc(s("inv_x"), 1)
                filler(n)

        def pe_recur(pe, h):
            rd = lambda key: pe.wait_ge(s("rec_done"), len(RD) * h + RD[key])
            pe.wait_ge(s("inv_x"), len(XD) * h + XD[LAST, 1, "XT"])
            for st in range(TT):
                for d in DIRS:
                    t = ORDER[d][st]
                    tile = slice(t * P, (t + 1) * P)
                    if st >= 1:
                        rd(("S", st - 1, d))
                        pe.matmul(bank(2 * d)[:, 0:P], kT[:, tile], state[d], start=True, stop=True
                                  ).then_inc(s("rec_mm"), 1)
                    if st >= CT:
                        q = slice((t - CT) * P, (t - CT + 1) * P)
                        pe.matmul(bank(4 + t - CT)[:, 0:P], qT_dec[d][:, q], state[d], start=(st == CT), stop=False)
                for d in DIRS:
                    t = ORDER[d][st]
                    if st >= 1:
                        rd(("r", st, d))
                    pe.matmul(bank(2 * d + 1)[:, 0:P], XTr[d][:, t, :], rest[d] if st else v_rows[:, t, :],
                              start=True, stop=True).then_inc(s("rec_mm"), 1)
                for d in DIRS:
                    t = ORDER[d][st]
                    if st < TT - 1:
                        rd(("vd", st, d))
                        pe.matmul(bank(2 * d)[:, 0:P], k_rows[:, t, :], v_dec[d], start=True, stop=True
                                  ).then_inc(s("rec_mm"), 1)
                    if st >= CT:
                        rd(("vn", st, d))
                        mm = pe.matmul(bank(4 + t - CT)[:, 0:P], QK[d][:, t - CT, :], v_new[d], start=False,
                                       stop=(st == TT - 1))
            mm.then_inc(s("o_done"), 1)

        def dve_recur(dve, h):
            rp = lambda key: dve.wait_ge(s("rec_mm"), len(RP) * h + RP[key])
            own = lambda key: dve.wait_ge(s("rec_done"), len(RD) * h + RD[key])
            done = lambda ins: ins.then_inc(s("rec_done"), 1)
            for st in range(TT):
                for d in DIRS:
                    t = ORDER[d][st]
                    if st >= 1:
                        rp(("kS", st, d))
                        done(dve.scalar_tensor_tensor(out=rest[d], in0=bank(2 * d)[:, 0:P], scalar=vec(neg_eg, t, d, h),
                                                      in1=v_rows[:, t, :], op0=ALU.mult, op1=ALU.add))
                for d in DIRS:
                    t = ORDER[d][st]
                    rp(("v", st, d))
                    if st < TT - 1:
                        done(dve.tensor_scalar(v_dec[d], bank(2 * d + 1)[:, 0:P], vec(bdec, t, d, h), None, ALU.mult))
                    if st >= CT:
                        done(dve.tensor_scalar(v_new[d], bank(2 * d + 1)[:, 0:P], vec(beta, t, d, h), None, ALU.mult))
                for d in DIRS:
                    t = ORDER[d][st]
                    if st < TT - 1:
                        rp(("S", st, d))
                        if st == 0:
                            done(dve.tensor_copy(state[d], bank(2 * d)[:, 0:P]))
                        else:
                            own(("S", st - 1, d))
                            done(dve.scalar_tensor_tensor(out=state[d], in0=state[d], scalar=vec(g_last, t, d, h),
                                                          in1=bank(2 * d)[:, 0:P], op0=ALU.mult, op1=ALU.add))

        def act_output_rows(act, h):
            act.wait_ge(s("o_done"), h + 1)
            act.copy(o_rows, m.ps[:, 4:6, 0:P]).then_inc(s("o_rows"), 1)

        def act_output_std(act, h):
            act.wait_ge(s("o_squares"), h + 1)
            act.activation(o_ss, o_ss, ACT.Sqrt, bias=v.l2_eps, scale=1.0 / P).then_inc(s("o_std"), 1)

        def dve_output(dve, h):
            dve.wait_ge(s("o_rows"), h + 1)
            dve.tensor_tensor(square_q, o_rows, o_rows, ALU.mult).then_inc(s("o_step"), 1)
            dve.wait_ge(s("o_step"), 3 * h + 1)
            dve.tensor_reduce(o_ss, square_q, AXX, ALU.add).then_inc(s("o_squares"), 1)
            dve.wait_ge(s("o_std"), h + 1)
            dve.reciprocal(o_rs, o_ss).then_inc(s("o_step"), 1)
            dve.wait_ge(s("o_step"), 3 * h + 2)
            dve.tensor_tensor(o_rows, o_rows, o_rs.unsqueeze(2).to_broadcast([P, XT, P]), ALU.mult
                              ).then_inc(s("o_step"), 1)
            dve.wait_ge(s("o_step"), 3 * h + 3)
            dve.wait_ge(s("z_gate"), h + 1)
            dve.tensor_tensor(o_rows, o_rows, z_gate, ALU.mult).then_inc(s("o_gated"), 1)

        def pe_output(pe, h, nxt):
            pe.wait_ge(s("o_gated"), h + 1)
            pe.wait_ge(s("proj_read"), 4 * nxt)
            for t in range(XT):
                mm = pe.transpose(bank(6)[:, t * P:(t + 1) * P], o_rows[:, t, :], v.ident)
            mm.then_inc(s("o_turned"), 1)

        def act_output(act, h):
            act.wait_ge(s("o_turned"), h + 1)
            act.copy(oT[:, bass.ds(h, 1), :].rearrange("p a n -> p (a n)"), bank(6)[:, 0:SEQ]).then_inc(s("oT"), 1)

        PE_FILL = {1: 0, 2: 1, 3: 2, 4: 3}
        DVE_FILL = {2: 0, 3: 1, 4: 2}

        def pe_head(pe, h, b, first=False, last=False):
            pe_prepare(pe, h)
            if not first:
                pe_output(pe, h - 1, h + 1)

            def filler(n):
                if n in PE_FILL and not last:
                    if n == 1 and not first:
                        pe.wait_ge(s("oT"), h)
                    pe_project(pe, h + 1, 1 - b, PE_FILL[n])
            pe_inverse(pe, h, filler)
            pe_recur(pe, h)
            if last:
                pe_output(pe, h, h + 1)

        def act_head(act, h, first=False, last=False):
            act_prepare_rows(act, h)
            if not first:
                act_output_std(act, h - 1)
            act_prepare(act, h)
            if not first:
                act_output(act, h - 1)
            if not last:
                for j in range(4):
                    act_project(act, h + 1, j)
                    if j >= 1:
                        act_conv(act, h + 1, j - 1)
            act_output_rows(act, h)
            if last:
                act_output_std(act, h)
                act_output(act, h)

        def dve_head(dve, h, first=False, last=False):
            if not first:
                dve_output(dve, h - 1)
            dve_prepare(dve, h)
            dve_inverse(dve, h, lambda n: dve_conv(dve, h + 1, DVE_FILL[n]) if n in DVE_FILL and not last else None)
            dve_recur(dve, h)
            if last:
                dve_output(dve, h)

        def heads(eng, one):
            one(0, 0, True, False)
            with eng.Fori(0, (HEADS - 2) // 2) as i:
                one(2 * i + 1, 1, False, False)
                one(2 * i + 2, 0, False, False)
            one(HEADS - 1, 1, False, True)

        def pe_dn_setup(pe):
            for n in range(2 * MT):
                t, half = divmod(n, 2)
                if half == 0:
                    pe.wait_ge(s("in1_h"), t + 1)
                if n >= 2:
                    pe.wait_ge(s("dn_hT"), 2 * (n - 1))
                for k in range(4):
                    mm = pe.transpose(m.ps[:, 6 + n % 2, k * P:(k + 1) * P],
                                      m.h[:, t, (4 * half + k) * P:(4 * half + k + 1) * P], v.ident)
                mm.then_inc(s("dn_turned"), 1)
            pe.wait_ge(s("dn_hT"), 4 * MT)
            pe.wait_ge(s("dn_small"), 16 * 5)
            pe.transpose(bank(5)[:, 0:CONV_ROWS], conv_rows, v.ident[0:CONV_ROWS, 0:CONV_ROWS]).then_inc(s("taps_turned"), 1)
            for k in range(KD):
                mm = pe.matmul(m.ps[0:2 * NV, 3, :], w_ab[:, k, :], m.hT[:, k, :], start=(k == 0), stop=(k == KD - 1))
            mm.then_inc(s("abT_mm"), 1)
            pe.wait_ge(s("abT"), 1)
            for t in range(TT):
                mm = pe.transpose(bank(4)[:, t * 2 * NV:(t + 1) * 2 * NV], abT[:, t * P:(t + 1) * P],
                                  v.ident[0:2 * NV, 0:2 * NV])
            mm.then_inc(s("ab_rows"), 1)
            for j in range(4):
                pe_project(pe, 0, 0, j)
            pe.wait_ge(s("log_decay"), 1)
            W = TT * NV
            pe.matmul(bank(3)[:, 0:W], v.upper_in, gate_a, start=True, stop=True)
            pe.matmul(bank(3)[:, W:2 * W], v.lower_in, gate_a, start=True, stop=True)
            pe.matmul(bank(3)[:, 2 * W:3 * W], v.ones, gate_a, start=True, stop=True).then_inc(s("cumulated"), 1)

        def act_dn_setup(act):
            for n in range(2 * MT):
                t, half = divmod(n, 2)
                act.wait_ge(s("dn_turned"), n + 1)
                src = m.ps[:, 6 + n % 2, :].rearrange("p (k n) -> p k n", k=4)
                for seg, c in ((CTX, 0), (0, HALF)):
                    act.copy(m.hT[:, 4 * half:4 * half + 4, seg + t * HALF:seg + (t + 1) * HALF], src[:, :, c:c + HALF]
                             ).then_inc(s("dn_hT"), 1)
            act.wait_ge(s("taps_turned"), 1)
            act.copy(taps[:, 0:CONV_ROWS], bank(5)[:, 0:CONV_ROWS]).then_inc(s("taps"), 1)
            act.wait_ge(s("abT_mm"), 1)
            act.copy(abT, m.ps[0:2 * NV, 3, :]).then_inc(s("abT"), 1)
            for j in range(4):
                act_project(act, 0, j)
            ab = bank(4)[:, 0:TT * 2 * NV].rearrange("p (t c) -> p t c", t=TT)
            act.wait_ge(s("gate_a"), 1)
            act.activation(beta.rearrange("p (t c) -> p t c", t=TT), ab[:, :, NV:2 * NV], ACT.Sigmoid
                           ).then_inc(s("beta"), 1)
            act.activation(soft, gate_a, ACT.Abs).then_inc(s("soft_step"), 1)
            act.wait_ge(s("soft_step"), 1)
            act.activation(soft, soft, ACT.Exp, scale=-1.0).then_inc(s("soft_step"), 1)
            act.wait_ge(s("soft_step"), 2)
            act.activation(soft, soft, ACT.Ln, bias=1.0).then_inc(s("soft_step"), 1)
            act.activation(a_neg, a_neg, ACT.Exp).then_inc(s("soft_step"), 1)
            act.wait_ge(s("cum_rows"), 1)
            act.activation(neg_eg, gc, ACT.Exp).then_inc(s("exps"), 1)
            act.activation(g_last, total, ACT.Exp).then_inc(s("exps"), 1)
            act.activation(bdec, bdec, ACT.Exp).then_inc(s("exps"), 1)
            for j in range(3):
                act_conv(act, 0, j)

        def dve_dn_setup(dve):
            for j in range(3):
                dve.memset(pad[j], 0.0).then_inc(s("pads"), 1)
            n = [0]

            def then(ins):
                n[0] += 1
                ins.then_inc(s("dn_step"), 1)
                dve.wait_ge(s("dn_step"), n[0])
            dve.wait_ge(s("dn_small"), 16 * 5)
            dve.wait_ge(s("ab_rows"), 1)
            ab = bank(4)[:, 0:TT * 2 * NV].rearrange("p (t c) -> p t c", t=TT)
            g3 = gate_a.rearrange("p (t c) -> p t c", t=TT)
            dve.tensor_tensor(g3, ab[:, :, 0:NV], dt_b.unsqueeze(1).to_broadcast([P, TT, NV]), ALU.add
                              ).then_inc(s("gate_a"), 1)
            dve.wait_ge(s("soft_step"), 4)
            then(dve.scalar_tensor_tensor(out=gate_a, in0=gate_a, scalar=0.0, in1=soft, op0=ALU.max, op1=ALU.add))
            dve.scalar_tensor_tensor(out=g3, in0=g3, scalar=-1.0, in1=a_neg.unsqueeze(1).to_broadcast([P, TT, NV]),
                                     op0=ALU.mult, op1=ALU.mult).then_inc(s("log_decay"), 1)
            dve.wait_ge(s("cumulated"), 1)
            W = TT * NV
            three = bank(3)[:, 0:3 * W].rearrange("p (a t c) -> p a t c", a=3, t=TT)
            gc3 = gc.rearrange("p (t c) -> p t c", t=TT)
            for d in DIRS:
                then(dve.tensor_copy(gc3[:, :, d * HEADS:(d + 1) * HEADS], three[:, d, :, d * HEADS:(d + 1) * HEADS]))
            then(dve.tensor_copy(total, bank(3)[:, 2 * W:3 * W]))
            dve.tensor_tensor(bdec, total, gc, ALU.subtract).then_inc(s("cum_rows"), 1)
            dve.wait_ge(s("exps"), 3)
            dve.wait_ge(s("beta"), 1)
            then(dve.tensor_scalar(neg_eg, neg_eg, -1.0, None, ALU.mult))
            then(dve.tensor_tensor(bdec, bdec, beta, ALU.mult))
            dve.wait_ge(s("taps"), 1)
            for j in range(3):
                dve_conv(dve, 0, j)

        def pe_dn_out(pe):
            pe.wait_ge(s("w_out"), 32)
            pe.wait_ge(s("oT"), HEADS)
            for t in range(XT):
                for half in range(2):
                    for h in range(HEADS):
                        mm = pe.matmul(bank(2 * t + half), oT[:, h, t * P:(t + 1) * P],
                                       w_out[h // 4][:, h % 4, half * BANK:(half + 1) * BANK],
                                       start=(h == 0), stop=(h == HEADS - 1))
                mm.then_inc(s("dn_y"), 1)

        def dn_y(t):
            return m.ps[:, 2 * t:2 * t + 2, :].rearrange("p a n -> p (a n)")

        def ln_loads(act, layer, sub):
            act.dma_start(m.ln[:, 0, :], in_ln_g[layer, sub].partition_broadcast(P)).then_inc(s("ln_vec"), 16)
            act.dma_start(m.ln[:, 1, :], in_ln_b[layer, sub].partition_broadcast(P)).then_inc(s("ln_vec"), 16)

        @block.sync
        def _(sp):
            sp_mod(sp, 0, 0, True)
            with sp.Fori(1, 4) as i:
                sp_mod(sp, i, 0, False)
            sp.wait_ge(s("mod_mm"), NCH)
            sp_moe(sp, L0)
            sp_moe_drained(sp, L0)
            for i in range(4, 8):
                sp_mod(sp, i, 1, False)
            sp.wait_ge(s("ln_normed"), 2 * MT)
            sp.wait_ge(s("mod_mm"), 2 * NCH)
            sp_heads_first(sp)
            for b in range(2):
                sp_head(sp, b, b)
            sp.dma_start(w_out[1], in_dn_w_out[0][4 * P:8 * P, :].rearrange("(h p) n -> p h n", p=P)).then_inc(s("w_out"), 16)
            sp.wait_ge(s("in1_h"), MT)
            for t in range(XT):
                sp.dma_start(m.x[HALF:P, 2 * t, :], m.x[0:HALF, 2 * t + 1, :]).then_inc(s("x_moved"), 16)
            sp.wait_ge(s("dn_turned"), 2 * MT)
            sp.dma_start(w_out[0], in_dn_w_out[0][0:4 * P, :].rearrange("(h p) n -> p h n", p=P)).then_inc(s("w_out"), 16)
            with sp.Fori(1, HEADS // 2) as i:
                for b in range(2):
                    sp.wait_ge(s("projected"), 8 * i + 4 * b - 4)
                    sp_head(sp, 2 * i + b, b)
            sp.wait_ge(s("projected"), 4 * HEADS)
            sp.wait_ge(s("dn_y"), XT)
            sp_moe(sp, L1)
            for n, t in enumerate(L1.x_tiles):
                sp.wait_ge(s("ln_x"), 2 * MT + XT + n + 1)
                sp.dma_start(out_dram[0, n * P:(n + 1) * P, :], m.x[:, t, :]).then_inc(s("stored"), 16)
            sp.wait_ge(s("stored"), 16 * XT)

        @block.gpsimd
        def _(pool):
            pool_mod(pool, 0, 0)
            with pool.Fori(1, 4) as i:
                pool_mod(pool, i, 0)
            for i in range(4, 8):
                pool_mod(pool, i, 1)
            pool.wait_ge(s("cum_rows"), 1)
            pool_head(pool, 0, True)
            pool_gate(pool, 0, True)
            with pool.Fori(1, HEADS) as h:
                pool_head(pool, h, False)
                pool_gate(pool, h, False)

        @block.scalar
        def _(act):
            act.dma_start(m.c_rows[0:KD, :], in_c[0].rearrange("(k p) -> k p", p=P)).then_inc(s("c_loaded"), 16)
            act.dma_start(m.c_rows[KD:2 * KD, :], in_c_ctx.rearrange("(k p) -> k p", p=P)).then_inc(s("c_loaded"), 16)
            act.dma_start(m.const[:, :], in_const).then_inc(s("const"), 16)
            act.dma_start(m.x[0:HALF, :, :], in_x[0].rearrange("(t p) d -> p t d", p=HALF)).then_inc(s("x_loaded"), 16)
            act.dma_start(m.x[HALF:P, :, :], in_ctx[0].rearrange("(t p) d -> p t d", p=HALF)).then_inc(s("x_loaded"), 16)
            act.dma_start(v.pool_scale, in_pool_scale[0].partition_broadcast(P)).then_inc(s("pool_scale"), 16)
            act.dma_start(v.pool_m, in_pool_m.rearrange("p w (t n) -> p w t n", t=MT)).then_inc(s("pool_m"), 16)
            act.dma_start(v.pool_w, in_pool_w[0].rearrange("w (c p) d -> p w c d", p=P)).then_inc(s("pool_w"), 16)
            ln_loads(act, 0, 0)
            act.dma_start(v.w_router, in_w_router.rearrange("(k p) e -> p k e", p=P)).then_inc(s("small_loads"), 16)
            act.dma_start(v.b_router, in_b_router.partition_broadcast(P)).then_inc(s("small_loads"), 16)
            act.wait_ge(s("c_loaded"), 32)
            act.activation(m.c_silu[:, :], m.c_rows[:, :], ACT.Silu).then_inc(s("c_silu"), 1)
            act_mod(act, 0, 0)
            act_mod(act, 1, 0)
            act_pool(act)
            for t in range(MT):
                act_norm(act, "ln0a_", t, t)
            with act.Fori(2, 4) as i:
                act_mod(act, i, 0)
            act.wait_ge(s("ln_x"), MT)
            ln_loads(act, 0, 1)
            act_router(act, L0)
            act_moe(act, L0)
            act_mod(act, 4, 1)
            for t in range(MT):
                act_norm(act, "ln0b_", t, t)
            act_mod(act, 5, 1)
            act_mod(act, 6, 1)
            act.wait_ge(s("ln_x"), 2 * MT)
            ln_loads(act, 1, 0)
            act_mod(act, 7, 1)
            act.wait_ge(s("pads"), 3)
            act_dn_setup(act)
            heads(act, lambda h, b, first, last: act_head(act, h, first, last))
            for t in range(XT):
                act_norm(act, "ln1a_", t, L1.x_tiles[t])
            act.wait_ge(s("ln_x"), 2 * MT + XT)
            ln_loads(act, 1, 1)
            act_router(act, L1)
            act_moe(act, L1)
            for t in range(XT):
                act_norm(act, "ln1b_", t, L1.x_tiles[t])

        @block.tensor
        def _(pe):
            pe.wait_ge(s("c_silu"), 1)
            pe.wait_ge(s("const"), 16)
            pe.transpose(m.ps[:, 7, 0:2 * KD], m.c_silu[:, :], v.ident[0:2 * KD, 0:2 * KD]).then_inc(s("c_turned"), 1)
            pe.wait_ge(s("c_spread"), 3)
            both = lambda i, j: v.c_mix
            pe_mod(pe, 0, both, True)
            pe_mod(pe, 1, both, False)
            pe_pool(pe)
            with pe.Fori(2, 4) as i:
                pe_mod(pe, i, both, False)
            pe_router(pe, L0)
            pe.wait_ge(s("mod_copied"), NCH)
            pe_moe(pe, L0)
            nt, tb = group_counts(pe, N_GROUPS - 1)
            pe.wait_ge(s(L0.tag + "summed"), 4 * tb + 4 * nt + 1)
            for i in range(4, 8):
                pe_mod(pe, i, lambda i, j: v.c_mix if 3 * (i - 4) + j < 4 else v.c_lat, False)
            pe_dn_setup(pe)
            heads(pe, lambda h, b, first, last: pe_head(pe, h, b, first, last))
            pe_dn_out(pe)
            pe_router(pe, L1)
            pe_moe(pe, L1)

        @block.vector
        def _(dve):
            dve.wait_ge(s("c_turned"), 1)
            cT = m.ps[:, 7, 0:2 * KD]
            lat = cT[:, 0:KD].unsqueeze(2).to_broadcast([P, KD, HALF])
            ctx_c = cT[:, KD:2 * KD].unsqueeze(2).to_broadcast([P, KD, HALF])
            dve.tensor_copy(v.c_mix[:, :, 0:HALF], lat).then_inc(s("c_spread"), 1)
            dve.tensor_copy(v.c_mix[:, :, HALF:P], ctx_c).then_inc(s("c_spread"), 1)
            dve.tensor_copy(v.c_lat, cT[:, 0:KD].unsqueeze(2).to_broadcast([P, KD, P])).then_inc(s("c_spread"), 1)

            def first_h(tag, biased):
                dve.wait_ge(s("mod_biased"), biased)
                for t in range(MT):
                    h = m.h[:, t, :]
                    dve.scalar_tensor_tensor(out=h, in0=mod_vec(SCALE1), scalar=1.0, in1=m.x[:, t, :],
                                             op0=ALU.add, op1=ALU.mult).then_inc(s(tag + "scaled"), 1)
                    dve.wait_ge(s(tag + "scaled"), t + 1)
                    dve.tensor_tensor(h, h, mod_vec(SHIFT1), ALU.add).then_inc(s(tag + "h"), 1)

            dve.wait_ge(s("x_loaded"), 32)
            first_h("in0_", 4)
            dve.wait_ge(s("mod_biased"), 6)
            dve.wait_ge(s("pool_scale"), 16)
            dve.tensor_tensor(mod_vec(GATE1), mod_vec(GATE1), v.pool_scale, ALU.mult).then_inc(s("pool_gate"), 1)
            dve.wait_ge(s("pool_gate"), 1)
            dve.wait_ge(s("const"), 16)
            for t in range(MT):
                dve_norm(dve, "ln0a_", t, t, pool_y, lambda n: dve.wait_ge(s("pool_y"), n + 1), mod_vec(GATE1),
                         None, lambda: dve.wait_ge(s("ln_vec"), 32))
            dve.wait_ge(s("mod_biased"), 10)
            for t in range(MT):
                dve_modulate(dve, "ln0a_", t, t, t, (SHIFT2, SCALE2))
            dve_router(dve, L0)
            dve_moe(dve, L0)
            dve.wait_ge(s("mod_biased"), NCH)
            dve.wait_ge(s("moe0_y_added"), 2)
            for t in range(MT):
                dve_norm(dve, "ln0b_", t, t, lambda n: v.y_rows[:, n, :], lambda n: None, mod_vec(GATE2),
                         None, lambda: dve.wait_ge(s("ln_vec"), 64))
            dve.wait_ge(s("ln_x"), 2 * MT)
            first_h("in1_", NCH + 4)
            dve_dn_setup(dve)
            heads(dve, lambda h, b, first, last: dve_head(dve, h, first, last))
            dve.wait_ge(s("mod_biased"), 2 * NCH)
            dve.wait_ge(s("x_moved"), 32)
            for t in range(XT):
                dve_norm(dve, "ln1a_", t, L1.x_tiles[t], dn_y, lambda n: dve.wait_ge(s("dn_y"), n + 1), mod_vec(GATE1),
                         None, lambda: dve.wait_ge(s("ln_vec"), 96))
            dve.wait_ge(s("dn_y"), XT)
            for t in range(XT):
                dve_modulate(dve, "ln1a_", t, L1.x_tiles[t], t, (SHIFT2, SCALE2))
            dve_router(dve, L1)
            dve_moe(dve, L1)
            dve.wait_ge(s("moe1_y_added"), 2)
            for t in range(XT):
                dve_norm(dve, "ln1b_", t, L1.x_tiles[t], lambda n: v.y_rows[:, n, :], lambda n: None, mod_vec(GATE2),
                         None, lambda: dve.wait_ge(s("ln_vec"), 128))


def constants():
    import numpy as np
    i, j = np.arange(P)[:, None], np.arange(P)[None, :]
    c = np.zeros((P, N_CONST * P), np.float32)

    def put(at, value):
        c[:, at * P:at * P + value.shape[1]] = value
    put(C_IDENT, i == j)
    put(C_ONES, np.ones((P, P)))
    put(C_UPPER, i < j)
    put(C_UPPER_IN, i <= j)
    put(C_LOWER_IN, i >= j)
    put(C_IOTA, np.tile(np.arange(1, MT * P + 1), (P, 1)))
    put(C_NEG_F, np.where(i <= j, 0.0, -1e30))
    put(C_NEG_B, np.where(i >= j, 0.0, -1e30))
    for n in range(LEVELS):
        b = 2 ** n
        joined = (i // (2 * b) == j // (2 * b)) & (i // b != j // b)
        put(C_LEVEL_F + n, joined & (i > j))
        put(C_LEVEL_B + n, joined & (i < j))

    def box(n, k):
        b = np.zeros((n, n))
        for t in range(n):
            lo, hi = max(t - k // 2, 0), min(t + k - k // 2, n)
            b[t, lo:hi] = 1.0 / (hi - lo)
        return b
    pool = np.zeros((NW, MT * P, MT * P), np.float32)
    n = np.arange(MT * P)
    lat = (n % P) < HALF
    place = (n // P) * HALF + n % HALF
    for w, k in enumerate(WINDOWS):
        grid = np.kron(box(SEQ // GRID_W, k), box(GRID_W, k))
        line = box(CTX, k)
        full = np.zeros((MT * P, MT * P))
        full[np.ix_(lat, lat)] = grid[np.ix_(place[lat], place[lat])]
        full[np.ix_(~lat, ~lat)] = line[np.ix_(place[~lat], place[~lat])]
        pool[w] = (full - np.eye(MT * P)).T
    pool = pool.reshape(NW, MT, P, MT * P).transpose(2, 0, 1, 3).reshape(P, NW, MT * MT * P)
    return c, np.ascontiguousarray(pool)


_INS = ["x", "c", "ctx", "c_ctx", "w_mod", "b_mod", "ln_g", "ln_b", "pool_w", "pool_scale", "dn_w_in", "dn_conv",
        "dn_a_log", "dn_dt_bias", "dn_norm", "dn_w_out", "w_router", "b_router", "w_gate", "w_up", "w_down"]


def kernel(**inputs):
    import numpy as _np
    import concourse.bacc as _bacc
    from concourse.bass_utils import run_bass_kernel_spmd as _run

    nc = _bacc.Bacc("TRN2", target_bir_lowering=False, num_devices=1)
    const, pool_m = constants()
    given = [(name, inputs[name]) for name in _INS] + [("const", const), ("pool_m", pool_m)]
    arrays, args = {}, []
    for name, a in given:
        a = _np.ascontiguousarray(a)
        arrays[f"in_{name}_dram"] = a
        args.append(nc.dram_tensor(f"in_{name}_dram", a.shape, F32, kind="ExternalInput").ap())
    args.append(nc.dram_tensor("out_dram", (1, SEQ, D), F32, kind="ExternalOutput").ap())
    build(nc, *args)
    return _run(nc, [arrays], core_ids=[0]).results[0]["out_dram"]
```

```python
import math
from contextlib import ExitStack

import concourse.bass as bass
from concourse import mybir

F32 = mybir.dt.float32
I32 = mybir.dt.int32
ALU = mybir.AluOpType
ACT = mybir.ActivationFunctionType
AXX = mybir.AxisListType.X

P = 128
D = 1024
KD = D // P
SEQ = 256
CTX = 256
GRID_W = 64
DEPTH = 2
HALF = P // 2
MT = SEQ // HALF
XT = SEQ // P
N_GROUPS = 4
PER_GROUP = 4
N_EXPERTS = N_GROUPS * PER_GROUP
FE = D // 4
FC = FE // P
WINDOWS = (2, 4, 8, 16)
NW = len(WINDOWS)
PG = D // NW
HEADS = 8
TAPS = 5
ALPHA = (2.0 * DEPTH) ** 0.25
LN_EPS = 1e-5
L2_EPS = 1e-6
BANK = 512
NCH = 6 * D // BANK
SHIFT1, SCALE1, GATE1, SHIFT2, SCALE2, GATE2 = range(6)
CONV_ROWS = TAPS * 3 * D // P

C_IDENT, C_ONES, C_UPPER, C_UPPER_IN, C_LOWER_IN, C_IOTA = 0, 1, 2, 3, 4, 5
C_NEG_F, C_NEG_B = 9, 10
C_LEVEL_F, C_LEVEL_B = 11, 18
N_CONST = 25
LEVELS = 7


def declare(nc, ctx):
    class Names:
        pass
    m = Names()

    def sb(name, shape, dt=F32):
        return ctx.enter_context(nc.sbuf_tensor(name, shape, dt))

    m.const = sb("const", [P, N_CONST * P])
    m.x = sb("x_rows", [P, MT, D])
    m.h = sb("h_rows", [P, MT, D])
    m.hT = sb("h_cols", [P, KD, MT * P])
    m.mod = sb("modulation", [P, 6 * D])
    m.bias = sb("mod_bias", [P, 3, BANK])
    m.ln = sb("ln_vectors", [P, 2, D])
    m.ring = sb("weight_ring", [P, 6, 2048])
    m.arena = sb("arena", [P, 14336])
    m.c_rows = sb("c_rows", [2 * KD, P])
    m.c_silu = sb("c_silu", [2 * KD, P])
    m.small = sb("small", [P, 768])
    m.meta = sb("tile_counts", [P, 8], I32)
    m.ps = ctx.enter_context(nc.psum_tensor("banks", [P, 8, BANK], F32))
    return m


def columns(m):
    class Names:
        pass
    v = Names()
    c = m.const
    v.ident = c[:, C_IDENT * P:(C_IDENT + 1) * P]
    v.ones = c[:, C_ONES * P:(C_ONES + 1) * P]
    v.upper = c[:, C_UPPER * P:(C_UPPER + 1) * P]
    v.upper_in = c[:, C_UPPER_IN * P:(C_UPPER_IN + 1) * P]
    v.lower_in = c[:, C_LOWER_IN * P:(C_LOWER_IN + 1) * P]
    a = m.arena
    v.pool_m = a[:, 0:8192].rearrange("p (w t n) -> p w t n", w=NW, t=MT)
    v.pool_w = a[:, 8192:10240].rearrange("p (w c n) -> p w c n", w=NW, c=PG // P)
    v.tmp = a[:, 10240:12288].rearrange("p (b n) -> p b n", b=2)
    v.c_mix = a[:, 12288:13312].rearrange("p (k n) -> p k n", k=KD)
    v.c_lat = a[:, 13312:14336].rearrange("p (k n) -> p k n", k=KD)
    v.pool_scale = m.hT[:, 0:2, :].rearrange("p a n -> p (a n)")
    v.slots_T = a[:, 0:4096].rearrange("p (k n) -> p k n", k=KD)
    v.slots_y = a[:, 4096:8192].rearrange("p (s n) -> p s n", s=MT)
    v.onehot = a[:, 8192:8704].rearrange("p (t n) -> p t n", t=MT)
    v.onehot_T = a[:, 8704:9216]
    v.hidden = a[:, 9216:9472].rearrange("p (f n) -> p f n", f=FC)
    v.silu = a[:, 9472:9728].rearrange("p (f n) -> p f n", f=FC)
    v.slot_w = a[:, 9728:9792].rearrange("p (s e) -> p s e", s=MT)
    v.logits_T = a[0:N_EXPERTS, 8192:8704]
    v.y_rows = m.hT[:, :, :].rearrange("p k n -> p (k n)").rearrange("p (t n) -> p t n", t=MT)
    v.mod_ring = [m.ring[:, 2 * j:2 * j + 2, :].rearrange("p a (b n) -> p (a b) n", b=4) for j in range(3)]
    s = m.small
    v.w_router = s[:, 0:128].rearrange("p (k e) -> p k e", k=KD)
    v.b_router = s[:, 128:144]
    v.scores = s[:, 144:208]
    v.sel = s[:, 208:272]
    v.pairs = s[:, 272:368]
    v.combine = s[:, 368:432]
    v.better = s[:, 432:496]
    v.compare = s[:, 496:544]
    v.group_sum = s[:, 544:560]
    v.group_hot = s[:, 560:576]
    v.key = s[:, 576:592]
    v.totals = s[:, 592:608]
    v.group_max = s[:, 608:612]
    v.weight_sum = s[:, 612:616]
    v.desc = s[:, 616:620]
    v.counts = s[:, 620:624]
    v.tiles_f = s[:, 624:632]
    v.stats = s[:, 632:656].rearrange("p (b n) -> p b n", b=4)
    v.mean_var = s[:, 656:660].rearrange("p (b n) -> p b n", b=2)
    v.std = s[:, 660:662]
    v.rstd = s[:, 662:664]
    v.shift_ln = s[:, 664:666]
    return v


class Layer:

    def __init__(self, n, tiles, x_tiles):
        self.n, self.tiles, self.x_tiles = n, tiles, x_tiles
        self.tag = f"moe{n}_"
        self.h_base = n * MT


def build(nc, in_x, in_c, in_ctx, in_c_ctx, in_w_mod, in_b_mod,
          in_ln_g, in_ln_b, in_pool_w, in_pool_scale, in_dn_w_in, in_dn_conv,
          in_dn_a_log, in_dn_dt_bias, in_dn_norm, in_dn_w_out, in_w_router, in_b_router,
          in_w_gate, in_w_up, in_w_down,
          in_const, in_pool_m, out_dram):
    with ExitStack() as ctx:
        m = declare(nc, ctx)
        v = columns(m)
        sems = {}

        def s(name):
            if name not in sems:
                sems[name] = ctx.enter_context(nc.semaphore(name))
            return sems[name]

        L0 = Layer(0, MT, tuple(range(MT)))
        L1 = Layer(1, XT, (0, 2))
        LN_BASE = {"ln0a_": 0, "ln0b_": MT, "ln1a_": 2 * MT, "ln1b_": 2 * MT + XT}
        H_BASE = {"ln0a_": 0, "ln1a_": MT}
        block = ctx.enter_context(nc.Block())

        def mod_vec(which):
            return m.mod[:, which * D:(which + 1) * D]

        def sp_mod(sp, i, layer, first):
            for j in range(3):
                n = 3 * (i - 4 * layer) + j
                if not first:
                    sp.wait_ge(s("mod_mm"), 3 * i + j - 2)
                sp.dma_start(v.mod_ring[j],
                             in_w_mod[layer].rearrange("(k p) n -> p k n", p=P)[:, :, bass.ds(n * BANK, BANK)]
                             ).then_inc(s(f"mod_w{j}"), 16)
                if not first:
                    sp.wait_ge(s("mod_biased"), 3 * i + j - 2)
                sp.dma_start(m.bias[:, j, :],
                             in_b_mod[layer][bass.ds(n * BANK, BANK)].partition_broadcast(P)
                             ).then_inc(s(f"mod_b{j}"), 16)

        def pe_mod(pe, i, lhs, first):
            for j in range(3):
                pe.wait_ge(s(f"mod_w{j}"), 16 * i + 16)
                if not first:
                    pe.wait_ge(s("mod_copied"), 3 * i + j - 2)
                for k in range(KD):
                    mm = pe.matmul(m.ps[:, j, :], lhs(i, j)[:, k, :], v.mod_ring[j][:, k, :],
                                   start=(k == 0), stop=(k == KD - 1))
                mm.then_inc(s("mod_mm"), 1)

        def act_mod(act, i, layer):
            for j in range(3):
                n = 3 * (i - 4 * layer) + j
                act.wait_ge(s("mod_mm"), 3 * i + j + 1)
                act.copy(m.mod[:, bass.ds(n * BANK, BANK)], m.ps[:, j, :]).then_inc(s("mod_copied"), 1)

        def pool_mod(pool, i, layer):
            for j in range(3):
                n = 3 * (i - 4 * layer) + j
                pool.wait_ge(s("mod_copied"), 3 * i + j + 1)
                pool.wait_ge(s(f"mod_b{j}"), 16 * i + 16)
                dst = m.mod[:, bass.ds(n * BANK, BANK)]
                pool.tensor_tensor(dst, dst, m.bias[:, j, :], ALU.add).then_inc(s("mod_biased"), 1)

        def dve_norm(dve, tag, n, xt, y, y_wait, gate, mod_next, ln_wait):
            b = n % 2
            c = LN_BASE[tag] + n
            x = m.x[:, xt, :]
            tmp = v.tmp[:, b, :]
            y_wait(n)
            if n >= 2:
                dve.wait_ge(s("ln_gained"), c - 1)
            dve.tensor_tensor(tmp, y(n), gate, ALU.mult).then_inc(s("ln_gated"), 1)
            dve.wait_ge(s("ln_gated"), c + 1)
            dve.scalar_tensor_tensor(out=x, in0=x, scalar=ALPHA, in1=tmp, op0=ALU.mult,
                                     op1=ALU.add).then_inc(s("ln_summed"), 1)
            dve.wait_ge(s("ln_summed"), c + 1)
            for half in range(2):
                dve.bn_stats(v.stats[:, 2 * b + half, :], x[:, half * BANK:(half + 1) * BANK]).then_inc(s("ln_stats"), 1)
            dve.wait_ge(s("ln_stats"), 2 * c + 2)
            dve.bn_aggr(v.mean_var[:, b, :], v.stats[:, 2 * b:2 * b + 2, :]).then_inc(s("ln_var"), 1)
            dve.wait_ge(s("ln_std"), c + 1)
            dve.reciprocal(v.rstd[:, b:b + 1], v.std[:, b:b + 1]).then_inc(s("ln_rstd"), 1)
            dve.wait_ge(s("ln_rstd"), c + 1)
            dve.scalar_tensor_tensor(out=v.shift_ln[:, b:b + 1], in0=v.mean_var[:, b, 0:1], scalar=-1.0,
                                     in1=v.rstd[:, b:b + 1], op0=ALU.mult, op1=ALU.mult
                                     ).then_inc(s("ln_centre"), 1)
            ln_wait()
            dve.wait_ge(s("ln_normed"), c + 1)
            dve.tensor_tensor(tmp, tmp, m.ln[:, 0, :], ALU.mult).then_inc(s("ln_gained"), 1)
            dve.wait_ge(s("ln_gained"), c + 1)
            dve.tensor_tensor(x, tmp, m.ln[:, 1, :], ALU.add).then_inc(s("ln_x"), 1)
            if mod_next is not None:
                dve_modulate(dve, tag, n, xt, n, mod_next)

        def dve_modulate(dve, tag, n, xt, ht, which):
            c = LN_BASE[tag] + n
            dve.wait_ge(s("ln_x"), c + 1)
            h = m.h[:, ht, :]
            hc = H_BASE[tag] + n
            dve.scalar_tensor_tensor(out=h, in0=mod_vec(which[1]), scalar=1.0, in1=m.x[:, xt, :],
                                     op0=ALU.add, op1=ALU.mult).then_inc(s("ln_h_scaled"), 1)
            dve.wait_ge(s("ln_h_scaled"), hc + 1)
            dve.tensor_tensor(h, h, mod_vec(which[0]), ALU.add).then_inc(s("ln_h"), 1)

        def act_norm(act, tag, n, xt):
            b = n % 2
            c = LN_BASE[tag] + n
            act.wait_ge(s("ln_var"), c + 1)
            act.activation(v.std[:, b:b + 1], v.mean_var[:, b, 1:2], ACT.Sqrt, bias=v.eps).then_inc(s("ln_std"), 1)
            act.wait_ge(s("ln_centre"), c + 1)
            act.activation(v.tmp[:, b, :], m.x[:, xt, :], ACT.Identity, bias=v.shift_ln[:, b:b + 1],
                           scale=v.rstd[:, b:b + 1]).then_inc(s("ln_normed"), 1)

        v.eps = LN_EPS
        v.l2_eps = L2_EPS
        v.const_iota = m.const[:, C_IOTA * P:(C_IOTA + MT) * P]

        w_gate_flat = in_w_gate.rearrange("l e d f -> (l e d) f")
        w_up_flat = in_w_up.rearrange("l e d f -> (l e d) f")
        w_down_flat = in_w_down.rearrange("l e f d -> (l e f) d")

        def expert_dst(half):
            r = m.ring
            return (r[:, 3 * half, :].rearrange("p (k f) -> p k f", k=KD),
                    r[:, 3 * half + 1, :].rearrange("p (k f) -> p k f", k=KD),
                    r[:, 3 * half + 2, :].rearrange("p (k f) -> p k f", k=FC))

        def sp_expert(sp, L, e, half):
            srcs = (w_gate_flat, w_up_flat, w_down_flat)
            for w, dst in zip(srcs, expert_dst(half)):
                rows = D if w is not w_down_flat else FE
                base = (L.n * N_EXPERTS + e) * rows
                src = w[bass.ds(base, rows), :].rearrange("(k p) f -> p k f", p=P)
                sp.dma_start(dst, src).then_inc(s(L.tag + f"w{half}"), 16)

        def group_counts(eng, g):
            nt = eng.value_load(m.meta[0:1, bass.ds(g, 1)], min_val=1, max_val=MT)
            tb = eng.value_load(m.meta[0:1, bass.ds(g + N_GROUPS, 1)], min_val=0, max_val=MT * N_GROUPS)
            return nt, tb

        def sp_moe(sp, L):
            for e in range(2):
                sp_expert(sp, L, e, e)
            sp.wait_ge(s(L.tag + "meta"), 1)

            def group(g, more):
                nt, tb = group_counts(sp, g)
                for e in range(2 + 2 * more):
                    sp.wait_ge(s(L.tag + "down"), 4 * tb + (e + 1) * nt)
                    sp_expert(sp, L, 4 * g + e + 2, e % 2)
            with sp.Fori(0, N_GROUPS - 1) as g:
                group(g, True)
            group(N_GROUPS - 1, False)

        def sp_moe_drained(sp, L):
            nt, tb = group_counts(sp, N_GROUPS - 1)
            sp.wait_ge(s(L.tag + "down"), 4 * tb + 4 * nt)

        def pe_router(pe, L):
            t_ = L.tag
            for n in range(2 * L.tiles):
                t, half = divmod(n, 2)
                if half == 0:
                    pe.wait_ge(s("ln_h"), L.h_base + t + 1)
                if n >= 2:
                    pe.wait_ge(s(t_ + "hT"), n - 1)
                for k in range(4):
                    mm = pe.transpose(m.ps[:, 6 + n % 2, k * P:(k + 1) * P],
                                      m.h[:, t, (4 * half + k) * P:(4 * half + k + 1) * P], v.ident)
                mm.then_inc(s(t_ + "turned"), 1)
            pe.wait_ge(s(t_ + "hT"), 2 * L.tiles)
            pe.wait_ge(s("small_loads"), 32)
            for k in range(KD):
                mm = pe.matmul(m.ps[0:N_EXPERTS, 4, 0:L.tiles * P], v.w_router[:, k, :],
                               m.hT[:, k, 0:L.tiles * P], start=(k == 0), stop=(k == KD - 1))
            mm.then_inc(s(t_ + "logits"), 1)
            pe.wait_ge(s(t_ + "logits_T"), 1)
            for t in range(L.tiles):
                mm = pe.transpose(m.ps[:, 5, t * N_EXPERTS:(t + 1) * N_EXPERTS], v.logits_T[:, t * P:(t + 1) * P],
                                  v.ident[0:N_EXPERTS, 0:N_EXPERTS])
            mm.then_inc(s(t_ + "logit_rows"), 1)
            pe.wait_ge(s(t_ + "group_hot"), 1)
            w = L.tiles * N_GROUPS
            pe.matmul(m.ps[:, 4, 0:w], v.upper, v.group_hot[:, 0:w], start=True, stop=True)
            pe.matmul(m.ps[:, 4, 16:16 + w], v.ones, v.group_hot[:, 0:w], start=True, stop=True
                      ).then_inc(s(t_ + "ranks"), 1)

        def act_router(act, L):
            t_ = L.tag
            for n in range(2 * L.tiles):
                t, half = divmod(n, 2)
                act.wait_ge(s(t_ + "turned"), n + 1)
                act.copy(m.hT[:, 4 * half:4 * half + 4, t * P:(t + 1) * P],
                         m.ps[:, 6 + n % 2, :].rearrange("p (k n) -> p k n", k=4)).then_inc(s(t_ + "hT"), 1)
            act.wait_ge(s(t_ + "logits"), 1)
            act.copy(v.logits_T[:, 0:L.tiles * P], m.ps[0:N_EXPERTS, 4, 0:L.tiles * P]).then_inc(s(t_ + "logits_T"), 1)
            act.wait_ge(s(t_ + "logit_rows"), 1)
            act.activation(v.scores[:, 0:L.tiles * N_EXPERTS], m.ps[:, 5, 0:L.tiles * N_EXPERTS],
                           ACT.Sigmoid).then_inc(s(t_ + "scores"), 1)

        def dve_router(dve, L):
            t_ = L.tag
            T, E, G, Q = L.tiles, N_EXPERTS, N_GROUPS, PER_GROUP
            step = [0]

            def then(ins):
                step[0] += 1
                ins.then_inc(s(t_ + "route_step"), 1)
                dve.wait_ge(s(t_ + "route_step"), step[0])

            scores = v.scores[:, 0:T * E]
            sel = v.sel[:, 0:T * E]
            by_group = sel.rearrange("p (a q) -> p a q", q=Q)
            then(dve.tensor_scalar(v.desc, v.const_iota[:, 0:G], -1.0, G + 1.0, ALU.mult, ALU.add))
            dve.wait_ge(s("small_loads"), 32)
            dve.wait_ge(s(t_ + "scores"), 1)
            then(dve.tensor_tensor(sel.rearrange("p (t e) -> p t e", t=T), scores.rearrange("p (t e) -> p t e", t=T),
                                   v.b_router.unsqueeze(1).to_broadcast([P, T, E]), ALU.add))
            pairs = v.pairs[:, 0:T * G * 6].rearrange("p (a q) -> p a q", q=6)
            at = 0
            for d in range(1, Q):
                ins = dve.tensor_tensor(pairs[:, :, at:at + Q - d], by_group[:, :, 0:Q - d], by_group[:, :, d:Q], ALU.add)
                then(ins)
                at += Q - d
            gsum = v.group_sum[:, 0:T * G]
            gsum3 = gsum.rearrange("p (t g) -> p t g", t=T)
            ghot = v.group_hot[:, 0:T * G]
            ghot3 = ghot.rearrange("p (t g) -> p t g", t=T)
            gmax = v.group_max[:, 0:T]
            gmax3 = gmax.unsqueeze(2).to_broadcast([P, T, G])
            then(dve.tensor_reduce(gsum, pairs, AXX, ALU.max))
            then(dve.tensor_reduce(gmax, gsum3, AXX, ALU.max))
            then(dve.tensor_tensor(ghot3, gsum3, gmax3, ALU.is_equal))
            then(dve.tensor_tensor(gsum3, ghot3, v.desc.unsqueeze(1).to_broadcast([P, T, G]), ALU.mult))
            then(dve.tensor_reduce(gmax, gsum3, AXX, ALU.max))
            dve.tensor_tensor(ghot3, gsum3, gmax3, ALU.is_equal).then_inc(s(t_ + "group_hot"), 1)
            dve.wait_ge(s(t_ + "group_hot"), 1)
            better = v.better[:, 0:T * E].rearrange("p (a q) -> p a q", q=Q)
            cmp = v.compare[:, 0:T * G * 3].rearrange("p (a q) -> p a q", q=3)
            then(dve.tensor_scalar(better, v.desc.unsqueeze(1).to_broadcast([P, T * G, Q]), -1.0, None, ALU.add))
            for d in range(1, Q):
                then(dve.tensor_tensor(cmp[:, :, 0:Q - d], by_group[:, :, 0:Q - d], by_group[:, :, d:Q], ALU.is_ge))
                then(dve.tensor_tensor(better[:, :, d:Q], better[:, :, d:Q], cmp[:, :, 0:Q - d], ALU.add))
                then(dve.tensor_tensor(better[:, :, 0:Q - d], better[:, :, 0:Q - d], cmp[:, :, 0:Q - d], ALU.subtract))
            comb = v.combine[:, 0:T * E]
            then(dve.tensor_scalar(better, better, 2.0, None, ALU.is_lt))
            then(dve.tensor_tensor(better, better, ghot.unsqueeze(2).to_broadcast([P, T * G, Q]), ALU.mult))
            then(dve.tensor_tensor(comb, scores, v.better[:, 0:T * E], ALU.mult))
            wsum = v.weight_sum[:, 0:T]
            then(dve.tensor_reduce(wsum, comb.rearrange("p (t e) -> p t e", t=T), AXX, ALU.add))
            then(dve.reciprocal(wsum, wsum))
            then(dve.tensor_tensor(comb.rearrange("p (t e) -> p t e", t=T), comb.rearrange("p (t e) -> p t e", t=T),
                                   wsum.unsqueeze(2).to_broadcast([P, T, E]), ALU.mult))
            dve.wait_ge(s(t_ + "ranks"), 1)
            key = v.key[:, 0:T * G]
            tot = v.totals[:, 0:T * G]
            then(dve.tensor_scalar(key, m.ps[:, 4, 0:T * G], 1.0, None, ALU.add))
            then(dve.tensor_copy(tot, m.ps[:, 4, 16:16 + T * G]))
            for t in range(1, T):
                for u in range(t):
                    then(dve.tensor_tensor(key[:, t * G:(t + 1) * G], key[:, t * G:(t + 1) * G],
                                           tot[:, u * G:(u + 1) * G], ALU.add))
            then(dve.tensor_tensor(key, key, ghot, ALU.mult))
            then(dve.tensor_reduce(v.counts, tot.rearrange("p (t g) -> p g t", t=T), AXX, ALU.add))
            tiles, before = v.tiles_f[:, 0:G], v.tiles_f[:, G:2 * G]
            then(dve.tensor_scalar(tiles, v.counts, float(P), 1.0, ALU.is_gt, ALU.add))
            for t in range(2, T):
                then(dve.scalar_tensor_tensor(out=tiles, in0=v.counts, scalar=float(t * P), in1=tiles,
                                              op0=ALU.is_gt, op1=ALU.add))
            then(dve.memset(before, 0.0))
            for g in range(1, G):
                then(dve.tensor_tensor(before[:, g:g + 1], before[:, g - 1:g], tiles[:, g - 1:g], ALU.add))
            dve.tensor_copy(m.meta[:, :], v.tiles_f).then_inc(s(t_ + "meta"), 1)
            dve.wait_ge(s(t_ + "meta"), 1)
            dve.memset(v.y_rows[:, 0:T, :], 0.0).then_inc(s(t_ + "y_added"), 1)

        def pe_moe(pe, L):
            t_ = L.tag
            T = L.tiles
            pe.wait_ge(s(t_ + "meta"), 1)
            with pe.Fori(0, N_GROUPS) as g:
                nt, tb = group_counts(pe, g)
                with pe.Fori(0, nt) as i:
                    q = tb + i
                    pe.wait_ge(s(t_ + "onehot"), q + 1)
                    pe.wait_ge(s(t_ + "slots_T_free"), 2 * q + 2)
                    for half in range(2):
                        for k in range(4):
                            for t in range(T):
                                mm = pe.matmul(m.ps[:, 6 + half, k * P:(k + 1) * P],
                                               m.h[:, t, (4 * half + k) * P:(4 * half + k + 1) * P],
                                               v.onehot[:, t, :], start=(t == 0), stop=(t == T - 1))
                        mm.then_inc(s(t_ + "gathered"), 1)
                    pe.wait_ge(s(t_ + "slot_w"), q + 1)
                    for t in range(T):
                        mm = pe.matmul(m.ps[:, 4, 0:N_EXPERTS], v.onehot[:, t, :],
                                       v.combine[:, t * N_EXPERTS:(t + 1) * N_EXPERTS],
                                       start=(t == 0), stop=(t == T - 1))
                    mm.then_inc(s(t_ + "weights_gathered"), 1)
                for e in range(PER_GROUP):
                    half = e % 2
                    wg, wu, wd = expert_dst(half)
                    with pe.Fori(0, nt) as i:
                        if e == 0:
                            pe.wait_ge(s(t_ + "slots_T_free"), 2 * tb + 2 * nt + 2)
                        pe.wait_ge(s(t_ + f"w{half}"), 96 * g + 48 * (e // 2) + 48)
                        q = 4 * tb + e * nt + i
                        for f in range(FC):
                            pe.wait_ge(s(t_ + "hidden"), 2 * q + f + 1)
                            for w, c in ((wg, 0), (wu, 1)):
                                for k in range(KD):
                                    mm = pe.matmul(m.ps[:, f, c * P:(c + 1) * P], w[:, k, f * P:(f + 1) * P],
                                                   v.slots_T[:, k, bass.ds(i * P, P)],
                                                   start=(k == 0), stop=(k == KD - 1))
                            mm.then_inc(s(t_ + "gate_up"), 1)
                        pe.wait_ge(s(t_ + "summed"), q + 1)
                        for f in range(FC):
                            pe.wait_ge(s(t_ + "hidden"), 2 * q + f + 3)
                            for half_d in range(2):
                                mm = pe.matmul(m.ps[:, 2 + half_d, :], v.hidden[:, f, :],
                                               wd[:, f, half_d * BANK:(half_d + 1) * BANK],
                                               start=(f == 0), stop=(f == FC - 1))
                        mm.then_inc(s(t_ + "down"), 1)
                with pe.Fori(0, nt) as i:
                    q = tb + i
                    pe.wait_ge(s(t_ + "onehot_again"), q + 1)
                    pe.wait_ge(s(t_ + "onehot_T"), q + 1)
                    for t in range(T):
                        mm = pe.transpose(m.ps[:, 5, t * P:(t + 1) * P], v.onehot[:, t, :], v.ident)
                    mm.then_inc(s(t_ + "onehot_turned"), 1)
                    pe.wait_ge(s(t_ + "onehot_T"), q + 2)
                    pe.wait_ge(s(t_ + "summed"), 4 * tb + 4 * nt + 1)
                    for n in range(2 * T):
                        t, half = divmod(n, 2)
                        pe.wait_ge(s(t_ + "y_added"), 2 * T * q + n + 1)
                        pe.matmul(m.ps[:, 6 + half, :], v.onehot_T[:, t * P:(t + 1) * P],
                                  v.slots_y[:, i, half * BANK:(half + 1) * BANK], start=True, stop=True
                                  ).then_inc(s(t_ + "spread"), 1)

        def act_moe(act, L):
            t_ = L.tag
            T = L.tiles
            act.wait_ge(s(t_ + "meta"), 1)
            act.sem_inc(s(t_ + "slots_T_free"), 2)
            act.sem_inc(s(t_ + "onehot_T"), 1)
            with act.Fori(0, N_GROUPS) as g:
                nt, tb = group_counts(act, g)
                with act.Fori(0, nt) as i:
                    q = tb + i
                    for half in range(2):
                        act.wait_ge(s(t_ + "gathered"), 2 * q + half + 1)
                        act.copy(v.slots_T[:, 4 * half:4 * half + 4, bass.ds(i * P, P)],
                                 m.ps[:, 6 + half, :].rearrange("p (k n) -> p k n", k=4)
                                 ).then_inc(s(t_ + "slots_T_free"), 1)
                for e in range(PER_GROUP):
                    with act.Fori(0, nt) as i:
                        q = 4 * tb + e * nt + i
                        for f in range(FC):
                            act.wait_ge(s(t_ + "gate_up"), 2 * q + f + 1)
                            act.activation(v.silu[:, f, :], m.ps[:, f, 0:P], ACT.Silu).then_inc(s(t_ + "silu"), 1)
                with act.Fori(0, nt) as i:
                    q = tb + i
                    act.wait_ge(s(t_ + "onehot_turned"), q + 1)
                    act.copy(v.onehot_T[:, 0:T * P], m.ps[:, 5, 0:T * P]).then_inc(s(t_ + "onehot_T"), 1)

        def dve_moe(dve, L):
            t_ = L.tag
            T = L.tiles
            dve.sem_inc(s(t_ + "y_added"), 1)
            dve.sem_inc(s(t_ + "slot_w"), 1)
            dve.sem_inc(s(t_ + "hidden"), 2)
            dve.sem_inc(s(t_ + "summed"), 1)

            def onehots(g, i, sem):
                for t in range(T):
                    ins = dve.tensor_scalar(v.onehot[:, t, :], v.const_iota[:, bass.ds(i * P, P)],
                                            v.key[:, bass.ds(g + t * N_GROUPS, 1)], None, ALU.is_equal)
                ins.then_inc(s(sem), 1)

            with dve.Fori(0, N_GROUPS) as g:
                nt, tb = group_counts(dve, g)
                with dve.Fori(0, nt) as i:
                    q = tb + i
                    onehots(g, i, t_ + "onehot")
                    dve.wait_ge(s(t_ + "weights_gathered"), q + 1)
                    dve.tensor_copy(v.slot_w[:, i, :], m.ps[:, 4, 0:N_EXPERTS]).then_inc(s(t_ + "slot_w"), 1)
                for e in range(PER_GROUP):
                    with dve.Fori(0, nt) as i:
                        q = 4 * tb + e * nt + i
                        for f in range(FC):
                            dve.wait_ge(s(t_ + "silu"), 2 * q + f + 1)
                            dve.tensor_tensor(v.hidden[:, f, :], v.silu[:, f, :], m.ps[:, f, P:2 * P], ALU.mult
                                              ).then_inc(s(t_ + "hidden"), 1)
                        dve.wait_ge(s(t_ + "down"), q + 1)
                        dve.wait_ge(s(t_ + "summed"), q + 1)
                        down = m.ps[:, 2:4, :].rearrange("p a n -> p (a n)")
                        w = v.slot_w[:, i, bass.ds(PER_GROUP * g + e, 1)]
                        y = v.slots_y[:, i, :]
                        if e == 0:
                            dve.wait_ge(s(t_ + "slot_w"), tb + nt + 1)
                            ins = dve.tensor_scalar(y, down, w, None, ALU.mult)
                        else:
                            ins = dve.scalar_tensor_tensor(out=y, in0=down, scalar=w, in1=y, op0=ALU.mult, op1=ALU.add)
                        ins.then_inc(s(t_ + "summed"), 1)
                with dve.Fori(0, nt) as i:
                    q = tb + i
                    onehots(g, i, t_ + "onehot_again")
                    for n in range(2 * T):
                        t, half = divmod(n, 2)
                        dve.wait_ge(s(t_ + "spread"), 2 * T * q + n + 1)
                        dst = v.y_rows[:, t, half * BANK:(half + 1) * BANK]
                        dve.wait_ge(s(t_ + "y_added"), 2 * T * q + n + 2)
                        dve.tensor_tensor(dst, dst, m.ps[:, 6 + half, :], ALU.add).then_inc(s(t_ + "y_added"), 1)

        def pe_pool(pe):
            for c in range(KD):
                if c == 0:
                    pe.wait_ge(s("in0_h"), MT)
                    pe.wait_ge(s("pool_m"), 16)
                if c >= 2:
                    pe.wait_ge(s("pooled_T"), c - 1)
                for t in range(MT):
                    mm = pe.matmul(m.ps[:, 3 + c % 2, :], m.h[:, t, c * P:(c + 1) * P], v.pool_m[:, c * P // PG, t, :],
                                   start=(t == 0), stop=(t == MT - 1))
                mm.then_inc(s("pooled"), 1)
            pe.wait_ge(s("pooled_T"), KD)
            pe.wait_ge(s("pool_w"), 16)
            for t in range(MT):
                if t >= 2:
                    pe.wait_ge(s("ln_gated"), t - 1)
                flat = m.ps[:, 3 + 2 * (t % 2):5 + 2 * (t % 2), :].rearrange("p a n -> p (a n)")
                for w in range(NW):
                    for c in range(PG // P):
                        mm = pe.matmul(flat[:, w * PG:(w + 1) * PG], m.hT[:, 2 * w + c, t * P:(t + 1) * P],
                                       v.pool_w[:, w, c, :], start=(c == 0), stop=(c == PG // P - 1))
                mm.then_inc(s("pool_y"), 1)

        def act_pool(act):
            act.wait_ge(s("pool_gate"), 1)
            for c in range(KD):
                act.wait_ge(s("pooled"), c + 1)
                act.copy(m.hT[:, c, :], m.ps[:, 3 + c % 2, :]).then_inc(s("pooled_T"), 1)

        def pool_y(t):
            return m.ps[:, 3 + 2 * (t % 2):5 + 2 * (t % 2), :].rearrange("p a n -> p (a n)")

        TT = (CTX + SEQ) // P
        CT = CTX // P
        ORDER = ((0, 1, 2, 3), (1, 0, 3, 2))
        a = m.arena
        at = [0]

        def take(n, shape=None, **kw):
            r = a[:, at[0]:at[0] + n]
            at[0] += n
            return r.rearrange(shape, **kw) if shape else r
        norm_g = take(128)
        taps = take(128)
        w_ab = take(256, "p (k n) -> p k n", k=KD)
        NV = 2 * HEADS
        gc, neg_eg, beta, bdec, g_last, gate_a, total, soft = [take(64) for _ in range(8)]
        dt_b, a_neg = take(16), take(16)
        pad = [take(2 * 260, "p (s n) -> p s n", s=2), take(2 * 260, "p (s n) -> p s n", s=2),
               take(260, "p (s n) -> p s n", s=1)]
        kT = [take(512) for _ in range(2)]
        qT = [take(256) for _ in range(2)]
        vT = take(512)
        k_rows = take(512, "p (t n) -> p t n", t=TT)
        v_rows = take(512, "p (t n) -> p t n", t=TT)
        q_square = take(256)
        square = take(256, "p (t n) -> p t n", t=XT)
        exp_q = take(512, "p (d n) -> p d n", d=2)
        qT_dec = [take(256) for _ in range(2)]
        decay = [take(512, "p (t n) -> p t n", t=TT) for _ in range(2)]
        NBT = [take(512, "p (t n) -> p t n", t=TT) for _ in range(2)]
        QK = [take(256, "p (t n) -> p t n", t=XT) for _ in range(2)]
        XTr = [take(512, "p (t n) -> p t n", t=TT) for _ in range(2)]
        Pm = [take(512, "p (t n) -> p t n", t=TT) for _ in range(2)]
        state = [take(128) for _ in range(2)]
        rest = [take(128) for _ in range(2)]
        v_new = [take(128) for _ in range(2)]
        v_dec = rest
        z_silu = take(256, "p (t n) -> p t n", t=XT)
        z_gate = take(256, "p (t n) -> p t n", t=XT)
        o_rows = take(256, "p (t n) -> p t n", t=XT)
        o_ss, o_rs = take(2), take(2)
        assert at[0] <= 13312, at[0]
        X = [take(512, "p (t n) -> p t n", t=TT) for _ in range(2)]
        assert at[0] <= 14336, at[0]
        conv_rows = k_rows.rearrange("p t n -> p (t n)")[0:CONV_ROWS, 0:P]
        abT = exp_q.rearrange("p d n -> p (d n)")[0:2 * NV, :]
        gcT = Pm[0][0:TT * NV, 0, :]
        along = m.x[:, 1, :].rearrange("p (d t n) -> p d t n", d=2, t=TT)
        k_square, norm = m.x[:, 3, 0:BANK], m.x[:, 3, BANK:2 * BANK]
        gc_dram = nc.dram_tensor("decay_rows", (TT * NV, P), F32).ap()
        oT = m.mod[:, 0:HEADS * SEQ].rearrange("p (h n) -> p h n", h=HEADS)
        head_w = [m.ring[:, 2 * b:2 * b + 2, :].rearrange("p a (c k n) -> p (a c) k n", c=2, k=KD) for b in range(2)]
        w_out = [m.h[:, :, :], m.ring[:, 4:6, :].rearrange("p a (c n) -> p (a c) n", c=2)]

        def vec(x, t, d, h):
            return x[:, bass.ds(t * NV + d * HEADS + h, 1)]

        def vecs(x, d, h):
            return x.rearrange("p (t c) -> p t c", t=TT)[:, :, bass.ds(d * HEADS + h, 1)].to_broadcast([P, TT, P])

        def marks(keys):
            return {k: n + 1 for n, k in enumerate(keys)}
        DIRS = (0, 1)
        LAST = LEVELS - 1
        RP = marks([(k, st, d) for st in range(TT) for k in ("kS", "v", "S") for d in DIRS
                    if not (k == "kS" and st == 0) and not (k == "S" and st == TT - 1)])
        RD = marks([(k, st, d) for st in range(TT) for ks in (("r",), ("vd", "vn"), ("S",)) for d in DIRS for k in ks
                    if not (k == "r" and st == 0) and not (k in ("vd", "S") and st == TT - 1)
                    and not (k == "vn" and st < CT)])

        def bank(n):
            return m.ps[:, n, :]

        def bank4(n):
            return m.ps[:, n, :].rearrange("p (t n) -> p t n", t=TT)

        def P_bank(d):
            return 3 * d

        def act_dn_small(act):
            act.dma_start(conv_rows, in_dn_conv[0].rearrange("j (c n) -> (j c) n", n=P)).then_inc(s("dn_small"), 16)
            act.dma_start(w_ab, in_dn_w_in[0].rearrange("(k p) n -> p k n", p=P)[:, :, 4 * D:4 * D + 2 * NV]
                         ).then_inc(s("dn_small"), 16)
            act.dma_start(dt_b, in_dn_dt_bias[0].rearrange("d h -> (d h)").partition_broadcast(P)).then_inc(s("dn_small"), 16)
            act.dma_start(a_neg, in_dn_a_log[0].rearrange("d h -> (d h)").partition_broadcast(P)).then_inc(s("dn_small"), 16)
            act.dma_start(norm_g, in_dn_norm[0].partition_broadcast(P)).then_inc(s("dn_small"), 16)

        def sp_head(sp, h, b):
            w = in_dn_w_in[0].rearrange("(k p) n -> p k n", p=P)
            for j, c in enumerate((1, 2, 0, 3)):
                sp.dma_start(head_w[b][:, j, :, :], w[:, :, bass.ds(c * D + h * P, P)]).then_inc(s(f"head_w{b}"), 16)

        SIDE = {"k_rows": (6, 0), "k+": (6, 1), "out-": (6, 2), "q+": (6, 3), "k_norm+": (6, 4),
                "q_norm+": (6, 5), "kk+": (6, 6), "v_rows": (7, 0), "v+": (7, 1), "z+": (7, 2), "qk+": (7, 3)}
        SIDE6, SIDE7 = 7, 4
        AHEAD6, AHEAD7 = 5, 3
        AHEAD = {"k+": 0, "v+": 0, "q+": 1, "z+": 1, "k_norm+": 2, "q_norm+": 3, "kk+": 4, "qk+": 2}
        SETUP = -1

        def side(key, h, use=None):
            b, n = SIDE[key]
            if isinstance(h, int) and h == SETUP:
                return b, AHEAD[key]
            per, ahead = (SIDE6, AHEAD6) if b == 6 else (SIDE7, AHEAD7)
            return b, per * h + ahead + (n if use is None else use)

        def side_free(pe, key, h, use=None):
            b, n = side(key, h, use)
            if not (isinstance(n, int) and n == 0):
                pe.wait_ge(s(f"side{b}_read"), n)

        def side_made(mm, key, h):
            mm.then_inc(s(f"side{side(key, h)[0]}_mm"), 1)

        def side_wait(eng, key, h, use=None):
            b, n = side(key, h, use)
            eng.wait_ge(s(f"side{b}_mm"), n + 1)

        def side_done(ins, key, h):
            ins.then_inc(s(f"side{side(key, h)[0]}_read"), 1)

        PROJ = ("k+", "v+", "q+", "z+")

        def pe_project(pe, h, b, j):
            nxt = h + 1
            if j == 0:
                pe.wait_ge(s(f"head_w{b}"), 64 * ((nxt - b) // 2) + 64 if isinstance(h, int) else 32 * (nxt - b) + 64)
            side_free(pe, PROJ[j], h)
            w = head_w[b][:, j, :, :]
            if j < 3:
                n0 = 0 if j < 2 else CTX
                for k in range(KD):
                    mm = pe.matmul(bank(6 + j % 2)[:, 0:CTX + SEQ - n0], w[:, k, :], m.hT[:, k, n0:CTX + SEQ],
                                   start=(k == 0), stop=(k == KD - 1))
            else:
                for t in range(XT):
                    for k in range(KD):
                        mm = pe.matmul(bank(7)[:, t * P:(t + 1) * P], m.hT[:, k, CTX + t * P:CTX + (t + 1) * P],
                                       w[:, k, :], start=(k == 0), stop=(k == KD - 1))
            side_made(mm, PROJ[j], h)

        def act_project(act, h, j):
            side_wait(act, PROJ[j], h)
            ahead = isinstance(h, int) and h == SETUP
            if j < 3:
                if not ahead:
                    act.wait_ge(s("conv_step"), 3 * TAPS * h + TAPS * (j + 1))
                n = 2 if j < 2 else 1
                side_done(act.copy(pad[j][:, :, 2:2 + SEQ], bank(6 + j % 2)[:, 0:n * SEQ].rearrange(
                    "p (s n) -> p s n", s=n)), PROJ[j], h)
            else:
                if not ahead:
                    act.wait_ge(s("z_gate"), h + 1)
                side_done(act.activation(z_silu, bank(7)[:, 0:SEQ].rearrange("p (t n) -> p t n", t=XT), ACT.Silu),
                          PROJ[j], h)

        def conv_out(j, b):
            return (kT[b], vT, qT[b])[j]

        def dve_conv(dve, h, b, j):
            bk, n_side = side(PROJ[j], h)
            dve.wait_ge(s(f"side{bk}_read"), n_side + 1)
            if j == 1 and not (isinstance(h, int) and h == SETUP):
                bk, n_side = side("v_rows", h)
                dve.wait_ge(s(f"side{bk}_read"), n_side + 1)
            n = 2 if j < 2 else 1
            out = conv_out(j, b).rearrange("p (s n) -> p s n", s=n)
            chunk = (HEADS, 2 * HEADS, 0)[j] + 1
            for c in range(TAPS):
                tap = taps[:, bass.ds(h + (c * 3 * HEADS + chunk), 1)]
                src = pad[j][:, :, c:c + SEQ]
                if c == 0:
                    ins = dve.tensor_scalar(out, src, tap, None, ALU.mult)
                else:
                    dve.wait_ge(s("conv_step"), 3 * TAPS * (h + 1) + TAPS * j + c)
                    ins = dve.scalar_tensor_tensor(out=out, in0=src, scalar=tap, in1=out, op0=ALU.mult, op1=ALU.add)
                ins.then_inc(s("conv_step"), 1)

        def act_conv(act, h, b, j):
            act.wait_ge(s("conv_step"), 3 * TAPS * (h + 1) + TAPS * (j + 1))
            act.activation(conv_out(j, b), conv_out(j, b), ACT.Silu).then_inc(s("conv_silu"), 1)

        def pool_square(pool, h, b, j, first=False):
            pool.wait_ge(s("conv_silu"), 3 * (h + 1) + (1, 0, 3)[j])
            if not (isinstance(h, int) and h == SETUP):
                side_wait(pool, ("k_norm+", None, "q_norm+")[j], SETUP if first else h - 1)
            src, dst = ((kT[b], k_square), None, (qT[b], q_square))[j]
            pool.tensor_tensor(dst, src, src, ALU.mult).then_inc(s("squares"), 1)

        def pe_norm(pe, h, j):
            key = ("k_norm+", None, "q_norm+")[j]
            side_free(pe, key, h)
            pe.wait_ge(s("squares"), 2 * (h + 1) + 1 + j // 2)
            src, n = ((k_square, 512), None, (q_square, 256))[j]
            side_made(pe.matmul(bank(6)[:, 0:n], v.ones, src, start=True, stop=True), key, h)

        def act_norm_root(act, h, j):
            key = ("k_norm+", None, "q_norm+")[j]
            side_wait(act, key, h)
            if j == 2:
                act.wait_ge(s("k_normed"), h + 2)
            elif not (isinstance(h, int) and h == SETUP):
                act.wait_ge(s("q_normed"), h + 1)
            n = 512 if j == 0 else 256
            side_done(act.activation(norm[:, 0:n], bank(6)[:, 0:n], ACT.Sqrt, bias=v.l2_eps), key, h)

        def dve_normed(dve, h, b, j):
            key = ("k_norm+", None, "q_norm+")[j]
            bk, n_side = side(key, h)
            dve.wait_ge(s(f"side{bk}_read"), n_side + 1)
            n = 512 if j == 0 else 256
            r = norm[:, 0:n]
            dve.reciprocal(r, r).then_inc(s("norm_step"), 1)
            dve.wait_ge(s("norm_step"), 2 * (h + 1) + 1 + j // 2)
            if j == 0:
                dve.tensor_tensor(kT[b], kT[b], r, ALU.mult).then_inc(s("k_normed"), 1)
            else:
                dve.scalar_tensor_tensor(out=qT[b], in0=r, scalar=float(P) ** -0.5, in1=qT[b], op0=ALU.mult,
                                         op1=ALU.mult).then_inc(s("q_normed"), 1)

        def sp_along(sp, h):
            if not (isinstance(h, int) and h == SETUP):
                sp.wait_ge(s("decay_exp"), 2 * (h + 1))
                sp.wait_ge(s("exp_q"), h + 1)
            rows = gc_dram.rearrange("(t d h) n -> h d t n", t=TT, d=2)[bass.ds(h + 1, 1)]
            for d in DIRS:
                sp.dma_start(along[:, d], rows[0, d].partition_broadcast(P)).then_inc(s("along"), 16)

        def dve_decay(dve, h):
            dve.wait_ge(s("along"), 32 * (h + 1) + 32)
            for d in DIRS:
                neg = m.const[:, (C_NEG_F + d) * P:(C_NEG_F + d + 1) * P].unsqueeze(1).to_broadcast([P, TT, P])
                dve.tensor_tensor(decay[d], along[:, d], neg, ALU.add).then_inc(s("decay_step"), 1)
            for d in DIRS:
                dve.wait_ge(s("decay_step"), 2 * (h + 1) + d + 1)
                dve.tensor_tensor(decay[d], decay[d], vecs(gc, d, h + 1), ALU.subtract).then_inc(s("decay_exp"), 1)

        def act_decay(act, h):
            act.wait_ge(s("along"), 32 * (h + 1) + 32)
            if not (isinstance(h, int) and h == SETUP):
                act.wait_ge(s("q_dec"), 2 * (h + 1))
            act.activation(exp_q.rearrange("p d (t n) -> p d t n", t=XT), along[:, :, CT:TT, :], ACT.Exp
                           ).then_inc(s("exp_q"), 1)
            for d in DIRS:
                act.wait_ge(s("decay_exp"), 2 * (h + 1) + d + 1)
                act.activation(decay[d], decay[d], ACT.Exp).then_inc(s("decay"), 1)

        def pe_products(pe, h, b, j):
            if j == 0:
                side_free(pe, "kk+", h)
                pe.wait_ge(s("k_normed"), h + 2)
                for t in range(TT):
                    mm = pe.matmul(bank(6)[:, t * P:(t + 1) * P], kT[b][:, t * P:(t + 1) * P],
                                   kT[b][:, t * P:(t + 1) * P], start=True, stop=True)
                side_made(mm, "kk+", h)
            else:
                side_free(pe, "qk+", h)
                pe.wait_ge(s("q_normed"), h + 2)
                for t in range(XT):
                    mm = pe.matmul(bank(7)[:, t * P:(t + 1) * P], kT[b][:, (CT + t) * P:(CT + t + 1) * P],
                                   qT[b][:, t * P:(t + 1) * P], start=True, stop=True)
                side_made(mm, "qk+", h)

        def dve_nbt(dve, h, d):
            side_wait(dve, "kk+", h)
            dve.wait_ge(s("decay"), 2 * (h + 1) + d + 1)
            ins = dve.tensor_tensor(NBT[d], decay[d], bank4(6), ALU.mult)
            if d == 0:
                ins.then_inc(s("nbt_step"), 1)
                dve.wait_ge(s("nbt_step"), h + 2)
            else:
                side_done(ins, "kk+", h)
                bk, n_side = side("kk+", h)
                dve.wait_ge(s(f"side{bk}_read"), n_side + 1)
            dve.tensor_tensor(NBT[d], NBT[d], vecs(beta, d, h + 1), ALU.mult).then_inc(s("nbt"), 1)

        def dve_queries(dve, h, b, first):
            side_wait(dve, "qk+", SETUP if first else h - 1)
            if not first:
                dve.wait_ge(s("o_done"), h)
            for d in DIRS:
                ins = dve.tensor_tensor(QK[d], decay[d][:, CT:TT, :],
                                        bank(7)[:, 0:SEQ].rearrange("p (t n) -> p t n", t=XT), ALU.mult)
            side_done(ins, "qk+", h)
            dve.wait_ge(s("exp_q"), h + 1)
            dve.wait_ge(s("q_normed"), h + 1)
            for d in DIRS:
                dve.tensor_tensor(qT_dec[d], qT[b], exp_q[:, d, :], ALU.mult).then_inc(s("q_dec"), 1)

        def pe_rows(pe, h, b, j):
            key = ("k_rows", "v_rows")[j]
            side_free(pe, key, h)
            if j == 1:
                pe.wait_ge(s("conv_silu"), 3 * h + 2)
            for t in range(TT):
                mm = pe.transpose(bank(6 + j)[:, t * P:(t + 1) * P], (kT[b], vT)[j][:, t * P:(t + 1) * P], v.ident)
            side_made(mm, key, h)

        def act_rows(act, h, j):
            key = ("k_rows", "v_rows")[j]
            side_wait(act, key, h)
            side_done(act.copy((k_rows, v_rows)[j], bank4(6 + j)), key, h)

        def pool_gate(pool, h, first):
            bk, n = side("z+", SETUP if first else h - 1)
            pool.wait_ge(s(f"side{bk}_read"), n + 1)
            if not first:
                pool.wait_ge(s("o_gated"), h)
            pool.tensor_tensor(z_gate, z_silu, norm_g.unsqueeze(1).to_broadcast([P, XT, P]), ALU.mult
                               ).then_inc(s("z_gate"), 1)

        def pe_inverse(pe, h, fill):
            def turn(n, d):
                pe.wait_ge(s("inv_x"), 2 * LEVELS * h + 2 * n + d + 1)
                for t in range(TT):
                    mm = pe.transpose(bank(P_bank(d) + 2)[:, t * P:(t + 1) * P], X[d][:, t, :], v.ident)
                mm.then_inc(s("inv_turned"), 1)

            for n in range(LEVELS):
                for d in DIRS:
                    if n == 0:
                        pe.wait_ge(s("nbt"), 2 * h + d + 1)
                    else:
                        pe.wait_ge(s("inv_x"), 2 * LEVELS * h + 2 * n + d - 1)
                    for t in range(TT):
                        out = bank(P_bank(d))[:, t * P:(t + 1) * P]
                        if n == 0:
                            mm = pe.transpose(out, NBT[d][:, t, :], v.ident)
                        else:
                            mm = pe.matmul(out, NBT[d][:, t, :], X[d][:, t, :], start=True, stop=True)
                    mm.then_inc(s("inv_p"), 1)
                    if n >= 1:
                        turn(n - 1, d)
                fill(n)
                if n == 0:
                    continue
                for d in DIRS:
                    pe.wait_ge(s("inv_pm"), 2 * LEVELS * h + 2 * n + d + 1)
                    pe.wait_ge(s("inv_xt"), 2 * LAST * h + 2 * n + d - 1)
                    l, r, out = (XTr[d], Pm[d], P_bank(d) + 1) if n < LAST else (Pm[d], XTr[d], P_bank(d) + 2)
                    for t in range(TT):
                        mm = pe.matmul(bank(out)[:, t * P:(t + 1) * P], l[:, t, :], r[:, t, :], start=True, stop=True)
                    mm.then_inc(s("inv_xp"), 1)

        def act_inverse(act, h, fill):
            for n in range(LAST):
                for d in DIRS:
                    act.wait_ge(s("inv_turned"), 2 * LAST * h + 2 * n + d + 1)
                    act.copy(XTr[d], bank4(P_bank(d) + 2)).then_inc(s("inv_xt"), 1)
                fill(n)

        def dve_inverse(dve, h, fill):
            for n in range(LEVELS):
                for d in DIRS:
                    level = m.const[:, ((C_LEVEL_F, C_LEVEL_B)[d] + n) * P:((C_LEVEL_F, C_LEVEL_B)[d] + n + 1) * P]
                    dve.wait_ge(s("inv_p"), 2 * LEVELS * h + 2 * n + d + 1)
                    dve.tensor_tensor(Pm[d], bank4(P_bank(d)), level.unsqueeze(1).to_broadcast([P, TT, P]), ALU.mult
                                      ).then_inc(s("inv_pm"), 1)
                for d in DIRS:
                    if n == 0:
                        dve.wait_ge(s("inv_pm"), 2 * LEVELS * h + d + 1)
                        ins = dve.tensor_tensor(X[d], v.ident.unsqueeze(1).to_broadcast([P, TT, P]), Pm[d], ALU.subtract)
                    else:
                        dve.wait_ge(s("inv_xp"), 2 * LAST * h + 2 * n + d - 1)
                        dst, b = (X[d], 1) if n < LAST else (XTr[d], 2)
                        ins = dve.tensor_tensor(dst, dst, bank4(P_bank(d) + b), ALU.subtract)
                    ins.then_inc(s("inv_x"), 1)
                fill(n)

        def pe_recur(pe, h, b, fill):
            rd = lambda key: pe.wait_ge(s("rec_done"), len(RD) * h + RD[key])
            pe.wait_ge(s("inv_x"), 2 * LEVELS * (h + 1))
            bk, n = side("v_rows", h)
            pe.wait_ge(s(f"side{bk}_read"), n + 1)
            for st in range(TT):
                for d in DIRS:
                    t = ORDER[d][st]
                    tile = slice(t * P, (t + 1) * P)
                    if st >= 1:
                        rd(("S", st - 1, d))
                        pe.matmul(bank(2 * d)[:, 0:P], kT[b][:, tile], state[d], start=True, stop=True
                                  ).then_inc(s("rec_mm"), 1)
                    if st >= CT:
                        q = slice((t - CT) * P, (t - CT + 1) * P)
                        pe.matmul(bank(4 + t - CT)[:, 0:P], qT_dec[d][:, q], state[d], start=(st == CT), stop=False)
                for d in DIRS:
                    t = ORDER[d][st]
                    if st >= 1:
                        rd(("r", st, d))
                    pe.matmul(bank(2 * d + 1)[:, 0:P], XTr[d][:, t, :], rest[d] if st else v_rows[:, t, :],
                              start=True, stop=True).then_inc(s("rec_mm"), 1)
                for d in DIRS:
                    t = ORDER[d][st]
                    if st < TT - 1:
                        rd(("vd", st, d))
                        pe.matmul(bank(2 * d)[:, 0:P], k_rows[:, t, :], v_dec[d], start=True, stop=True
                                  ).then_inc(s("rec_mm"), 1)
                    if st >= CT:
                        rd(("vn", st, d))
                        mm = pe.matmul(bank(4 + t - CT)[:, 0:P], QK[d][:, t - CT, :], v_new[d], start=False,
                                       stop=(st == TT - 1))
                if st < TT - 1:
                    fill(st)
            mm.then_inc(s("o_done"), 1)

        def dve_recur(dve, h, fill):
            rp = lambda key: dve.wait_ge(s("rec_mm"), len(RP) * h + RP[key])
            own = lambda key: dve.wait_ge(s("rec_done"), len(RD) * h + RD[key])
            done = lambda ins: ins.then_inc(s("rec_done"), 1)
            for st in range(TT):
                for d in DIRS:
                    t = ORDER[d][st]
                    if st >= 1:
                        rp(("kS", st, d))
                        done(dve.scalar_tensor_tensor(out=rest[d], in0=bank(2 * d)[:, 0:P], scalar=vec(neg_eg, t, d, h),
                                                      in1=v_rows[:, t, :], op0=ALU.mult, op1=ALU.add))
                for d in DIRS:
                    t = ORDER[d][st]
                    rp(("v", st, d))
                    if st < TT - 1:
                        done(dve.tensor_scalar(v_dec[d], bank(2 * d + 1)[:, 0:P], vec(bdec, t, d, h), None, ALU.mult))
                    if st >= CT:
                        done(dve.tensor_scalar(v_new[d], bank(2 * d + 1)[:, 0:P], vec(beta, t, d, h), None, ALU.mult))
                for d in DIRS:
                    t = ORDER[d][st]
                    if st < TT - 1:
                        rp(("S", st, d))
                        if st == 0:
                            done(dve.tensor_copy(state[d], bank(2 * d)[:, 0:P]))
                        else:
                            own(("S", st - 1, d))
                            done(dve.scalar_tensor_tensor(out=state[d], in0=state[d], scalar=vec(g_last, t, d, h),
                                                          in1=bank(2 * d)[:, 0:P], op0=ALU.mult, op1=ALU.add))
                fill(st)

        def act_output_rows(act, h):
            act.wait_ge(s("o_done"), h + 1)
            act.copy(o_rows, m.ps[:, 4:6, 0:P]).then_inc(s("o_rows"), 1)

        def act_output_std(act, h):
            act.wait_ge(s("o_squares"), h + 1)
            act.activation(o_ss, o_ss, ACT.Sqrt, bias=v.l2_eps, scale=1.0 / P).then_inc(s("o_std"), 1)

        def dve_output_squares(dve, h):
            dve.wait_ge(s("o_rows"), h + 1)
            dve.tensor_tensor(square, o_rows, o_rows, ALU.mult).then_inc(s("o_step"), 1)
            dve.wait_ge(s("o_step"), 3 * h + 1)
            dve.tensor_reduce(o_ss, square, AXX, ALU.add).then_inc(s("o_squares"), 1)

        def dve_output(dve, h):
            dve.wait_ge(s("o_std"), h + 1)
            dve.reciprocal(o_rs, o_ss).then_inc(s("o_step"), 1)
            dve.wait_ge(s("o_step"), 3 * h + 2)
            dve.tensor_tensor(o_rows, o_rows, o_rs.unsqueeze(2).to_broadcast([P, XT, P]), ALU.mult
                              ).then_inc(s("o_step"), 1)
            dve.wait_ge(s("o_step"), 3 * h + 3)
            dve.wait_ge(s("z_gate"), h + 1)
            dve.tensor_tensor(o_rows, o_rows, z_gate, ALU.mult).then_inc(s("o_gated"), 1)

        def pe_output(pe, h, use=None):
            side_free(pe, "out-", h, use)
            pe.wait_ge(s("o_gated"), h)
            for t in range(XT):
                mm = pe.transpose(bank(6)[:, t * P:(t + 1) * P], o_rows[:, t, :], v.ident)
            side_made(mm, "out-", h)

        def act_output(act, h, use=None):
            side_wait(act, "out-", h, use)
            side_done(act.copy(oT[:, bass.ds(h - 1, 1), :].rearrange("p a n -> p (a n)"), bank(6)[:, 0:SEQ]),
                      "out-", h)

        def pe_head(pe, h, b, first=False, last=False):
            def beside(n):
                if n == 0:
                    pe_rows(pe, h, b, 0)
                if n == 1:
                    pe_rows(pe, h, b, 1)
                if n == 2 and last:
                    pe_output(pe, h, 1)
                if last:
                    return
                if n in (1, 2, 3, 5):
                    pe_project(pe, h, 1 - b, (1, 2, 3, 5).index(n))
                if n == 5:
                    pe_norm(pe, h, 2)
                if n == 2:
                    if first:
                        pe.sem_inc(s("side6_mm"), 1)
                    else:
                        pe_output(pe, h)
                if n == 4:
                    pe_norm(pe, h, 0)
            if not first:
                pe.wait_ge(s("o_rows"), h)
            pe_inverse(pe, h, beside)
            pe_recur(pe, h, b, lambda st: pe_products(pe, h, 1 - b, st) if st < 2 and not last else None)
            if last:
                pe_output(pe, h + 1, 2 - SIDE6)

        def act_head(act, h, b, first=False, last=False):
            act_rows(act, h, 0)

            def beside(n):
                if n == 0:
                    act_rows(act, h, 1)
                    if not first:
                        act_output_std(act, h - 1)
                if n == 1 and last:
                    act_output(act, h, 1)
                if last:
                    return
                if n < 2:
                    act_project(act, h, n)
                if n == 1:
                    act_conv(act, h, 1 - b, 0)
                    if first:
                        act.wait_ge(s("side6_mm"), side("out-", h)[1] + 1)
                        act.sem_inc(s("side6_read"), 1)
                    else:
                        act_output(act, h)
                if n == 2:
                    act_project(act, h, 2)
                    act_conv(act, h, 1 - b, 1)
                    act_decay(act, h)
                if n == 3:
                    act_conv(act, h, 1 - b, 2)
                    act_norm_root(act, h, 0)
                if n == 4:
                    act_norm_root(act, h, 2)
                if n == 5:
                    act_project(act, h, 3)
            act_inverse(act, h, beside)
            act_output_rows(act, h)
            if last:
                act_output_std(act, h)
                act_output(act, h + 1, 2 - SIDE6)

        def dve_head(dve, h, b, first=False, last=False):
            def beside(n):
                if n == 0:
                    dve_queries(dve, h, b, first)
                    if not first:
                        dve_output_squares(dve, h - 1)
                if n in (1, 2, 3) and not last:
                    dve_conv(dve, h, 1 - b, n - 1)
                if n == 1 and not first:
                    dve_output(dve, h - 1)
                if last:
                    return
                if n == 1:
                    dve_decay(dve, h)
                if n in (4, 5):
                    dve_normed(dve, h, 1 - b, 2 * (n - 4))
            dve_inverse(dve, h, beside)
            dve_recur(dve, h, lambda st: dve_nbt(dve, h, st - 2) if st >= 2 and not last else None)
            if last:
                dve_output_squares(dve, h)
                dve_output(dve, h)

        def pool_head(pool, h, b, first=False, last=False):
            pool_gate(pool, h, first)
            if not last:
                pool_square(pool, h, 1 - b, 0, first)
                pool_square(pool, h, 1 - b, 2, first)

        def heads(eng, one):
            one(eng, 0, 0, first=True)
            with eng.Fori(0, (HEADS - 2) // 2) as i:
                one(eng, 2 * i + 1, 1)
                one(eng, 2 * i + 2, 0)
            one(eng, HEADS - 1, 1, last=True)

        def pe_dn_setup(pe):
            for n in range(2 * MT):
                t, half = divmod(n, 2)
                if half == 0:
                    pe.wait_ge(s("in1_h"), t + 1)
                if n >= 2:
                    pe.wait_ge(s("dn_hT"), 2 * (n - 1))
                for k in range(4):
                    mm = pe.transpose(m.ps[:, 6 + n % 2, k * P:(k + 1) * P],
                                      m.h[:, t, (4 * half + k) * P:(4 * half + k + 1) * P], v.ident)
                mm.then_inc(s("dn_turned"), 1)
            pe.wait_ge(s("dn_hT"), 4 * MT)
            pe.wait_ge(s("dn_small"), 16 * 5)
            pe.transpose(bank(5)[:, 0:CONV_ROWS], conv_rows, v.ident[0:CONV_ROWS, 0:CONV_ROWS]).then_inc(s("taps_turned"), 1)
            for k in range(KD):
                mm = pe.matmul(m.ps[0:2 * NV, 3, :], w_ab[:, k, :], m.hT[:, k, :], start=(k == 0), stop=(k == KD - 1))
            mm.then_inc(s("abT_mm"), 1)
            pe.wait_ge(s("abT"), 1)
            for t in range(TT):
                mm = pe.transpose(bank(4)[:, t * 2 * NV:(t + 1) * 2 * NV], abT[:, t * P:(t + 1) * P],
                                  v.ident[0:2 * NV, 0:2 * NV])
            mm.then_inc(s("ab_rows"), 1)

        def pe_dn_cumulate(pe):
            pe.wait_ge(s("log_decay"), 1)
            W = TT * NV
            pe.matmul(bank(3)[:, 0:W], v.upper_in, gate_a, start=True, stop=True)
            pe.matmul(bank(3)[:, W:2 * W], v.lower_in, gate_a, start=True, stop=True)
            pe.matmul(bank(3)[:, 2 * W:3 * W], v.ones, gate_a, start=True, stop=True).then_inc(s("cumulated"), 1)
            pe.wait_ge(s("cum_rows"), 1)
            pe.wait_ge(s("taps"), 1)
            pe.transpose(bank(5)[0:W, 0:P], gc, v.ident).then_inc(s("gc_turned"), 1)

        def pe_dn_first(pe):
            for j in range(4):
                pe_project(pe, SETUP, 0, j)
            for j in (0, 2):
                pe_norm(pe, SETUP, j)
            for j in range(2):
                pe_products(pe, SETUP, 0, j)

        def act_dn_setup(act):
            for n in range(2 * MT):
                t, half = divmod(n, 2)
                act.wait_ge(s("dn_turned"), n + 1)
                src = m.ps[:, 6 + n % 2, :].rearrange("p (k n) -> p k n", k=4)
                for seg, c in ((CTX, 0), (0, HALF)):
                    act.copy(m.hT[:, 4 * half:4 * half + 4, seg + t * HALF:seg + (t + 1) * HALF], src[:, :, c:c + HALF]
                             ).then_inc(s("dn_hT"), 1)
            act.wait_ge(s("taps_turned"), 1)
            act.copy(taps[:, 0:CONV_ROWS], bank(5)[:, 0:CONV_ROWS]).then_inc(s("taps"), 1)
            act.wait_ge(s("abT_mm"), 1)
            act.copy(abT, m.ps[0:2 * NV, 3, :]).then_inc(s("abT"), 1)
            ab = bank(4)[:, 0:TT * 2 * NV].rearrange("p (t c) -> p t c", t=TT)
            act.wait_ge(s("gate_a"), 1)
            act.activation(beta.rearrange("p (t c) -> p t c", t=TT), ab[:, :, NV:2 * NV], ACT.Sigmoid
                           ).then_inc(s("beta"), 1)
            act.activation(soft, gate_a, ACT.Abs).then_inc(s("soft_step"), 1)
            act.wait_ge(s("soft_step"), 1)
            act.activation(soft, soft, ACT.Exp, scale=-1.0).then_inc(s("soft_step"), 1)
            act.wait_ge(s("soft_step"), 2)
            act.activation(soft, soft, ACT.Ln, bias=1.0).then_inc(s("soft_step"), 1)
            act.activation(a_neg, a_neg, ACT.Exp).then_inc(s("soft_step"), 1)

        def act_dn_exps(act):
            act.wait_ge(s("gc_turned"), 1)
            act.copy(gcT, bank(5)[0:TT * NV, 0:P]).then_inc(s("gcT"), 1)
            act.activation(neg_eg, gc, ACT.Exp).then_inc(s("exps"), 1)
            act.activation(g_last, total, ACT.Exp).then_inc(s("exps"), 1)
            act.activation(bdec, bdec, ACT.Exp).then_inc(s("exps"), 1)

        def act_dn_first(act):
            act_project(act, SETUP, 0)
            for j in range(3):
                act_project(act, SETUP, j + 1)
                act_conv(act, SETUP, 0, j)
            for j in (0, 2):
                act_norm_root(act, SETUP, j)
            act_decay(act, SETUP)

        def dve_dn_setup(dve):
            for j in range(3):
                dve.memset(pad[j], 0.0).then_inc(s("pads"), 1)
            n = [0]

            def then(ins):
                n[0] += 1
                ins.then_inc(s("dn_step"), 1)
                dve.wait_ge(s("dn_step"), n[0])
            dve.wait_ge(s("dn_small"), 16 * 5)
            dve.wait_ge(s("ab_rows"), 1)
            ab = bank(4)[:, 0:TT * 2 * NV].rearrange("p (t c) -> p t c", t=TT)
            g3 = gate_a.rearrange("p (t c) -> p t c", t=TT)
            dve.tensor_tensor(g3, ab[:, :, 0:NV], dt_b.unsqueeze(1).to_broadcast([P, TT, NV]), ALU.add
                              ).then_inc(s("gate_a"), 1)
            dve.wait_ge(s("soft_step"), 4)
            then(dve.scalar_tensor_tensor(out=gate_a, in0=gate_a, scalar=0.0, in1=soft, op0=ALU.max, op1=ALU.add))
            dve.scalar_tensor_tensor(out=g3, in0=g3, scalar=-1.0, in1=a_neg.unsqueeze(1).to_broadcast([P, TT, NV]),
                                     op0=ALU.mult, op1=ALU.mult).then_inc(s("log_decay"), 1)
            dve.wait_ge(s("cumulated"), 1)
            W = TT * NV
            three = bank(3)[:, 0:3 * W].rearrange("p (a t c) -> p a t c", a=3, t=TT)
            gc3 = gc.rearrange("p (t c) -> p t c", t=TT)
            for d in DIRS:
                then(dve.tensor_copy(gc3[:, :, d * HEADS:(d + 1) * HEADS], three[:, d, :, d * HEADS:(d + 1) * HEADS]))
            then(dve.tensor_copy(total, bank(3)[:, 2 * W:3 * W]))
            dve.tensor_tensor(bdec, total, gc, ALU.subtract).then_inc(s("cum_rows"), 1)
            dve.wait_ge(s("exps"), 3)
            dve.wait_ge(s("beta"), 1)
            then(dve.tensor_scalar(neg_eg, neg_eg, -1.0, None, ALU.mult))
            then(dve.tensor_tensor(bdec, bdec, beta, ALU.mult))
            dve.wait_ge(s("taps"), 1)
            for j in range(3):
                dve_conv(dve, SETUP, 0, j)
            for j in (0, 2):
                dve_normed(dve, SETUP, 0, j)
            dve_decay(dve, SETUP)
            for d in DIRS:
                dve_nbt(dve, SETUP, d)

        def pe_dn_out(pe):
            pe.wait_ge(s("w_out"), 32)
            pe.wait_ge(s("side6_read"), SIDE6 * (HEADS - 1) + AHEAD6 + 3)
            for t in range(XT):
                for half in range(2):
                    for h in range(HEADS):
                        mm = pe.matmul(bank(2 * t + half), oT[:, h, t * P:(t + 1) * P],
                                       w_out[h // 4][:, h % 4, half * BANK:(half + 1) * BANK],
                                       start=(h == 0), stop=(h == HEADS - 1))
                mm.then_inc(s("dn_y"), 1)

        def dn_y(t):
            return m.ps[:, 2 * t:2 * t + 2, :].rearrange("p a n -> p (a n)")

        def ln_loads(act, layer, sub):
            act.dma_start(m.ln[:, 0, :], in_ln_g[layer, sub].partition_broadcast(P)).then_inc(s("ln_vec"), 16)
            act.dma_start(m.ln[:, 1, :], in_ln_b[layer, sub].partition_broadcast(P)).then_inc(s("ln_vec"), 16)

        @block.sync
        def _(sp):
            sp_mod(sp, 0, 0, True)
            with sp.Fori(1, 4) as i:
                sp_mod(sp, i, 0, False)
            sp.wait_ge(s("mod_mm"), NCH)
            sp_moe(sp, L0)
            sp_moe_drained(sp, L0)
            for i in range(4, 8):
                sp_mod(sp, i, 1, False)
            sp.wait_ge(s("in1_h"), MT)
            for t in range(XT):
                sp.dma_start(m.x[HALF:P, 2 * t, :], m.x[0:HALF, 2 * t + 1, :]).then_inc(s("x_moved"), 16)
            sp.wait_ge(s("gcT"), 1)
            sp.dma_start(gc_dram, gcT).then_inc(s("gc_rows"), 16)
            sp.wait_ge(s("gc_rows"), 16)
            sp.wait_ge(s("x_moved"), 32)
            sp_along(sp, SETUP)
            for b in range(2):
                sp.wait_ge(s("mod_mm"), 2 * NCH - 2 + b)
                sp_head(sp, b, b)
            sp.wait_ge(s("mod_mm"), 2 * NCH)
            sp.dma_start(w_out[1], in_dn_w_out[0][4 * P:8 * P, :].rearrange("(h p) n -> p h n", p=P)).then_inc(s("w_out"), 16)
            sp.wait_ge(s("dn_turned"), 2 * MT)
            sp.dma_start(w_out[0], in_dn_w_out[0][0:4 * P, :].rearrange("(h p) n -> p h n", p=P)).then_inc(s("w_out"), 16)
            sp_along(sp, 0)
            with sp.Fori(1, HEADS // 2) as i:
                for b in range(2):
                    sp.wait_ge(s("side7_mm"), SIDE7 * (2 * i + b - 3) + AHEAD7 + 3)
                    sp_head(sp, 2 * i + b, b)
                    sp_along(sp, 2 * i + b - 1)
            sp.wait_ge(s("dn_y"), XT)
            sp_moe(sp, L1)
            for n, t in enumerate(L1.x_tiles):
                sp.wait_ge(s("ln_x"), 2 * MT + XT + n + 1)
                sp.dma_start(out_dram[0, n * P:(n + 1) * P, :], m.x[:, t, :]).then_inc(s("stored"), 16)
            sp.wait_ge(s("stored"), 16 * XT)

        @block.gpsimd
        def _(pool):
            pool_mod(pool, 0, 0)
            with pool.Fori(1, 4) as i:
                pool_mod(pool, i, 0)
            for i in range(4, 8):
                pool_mod(pool, i, 1)
            pool.wait_ge(s("cum_rows"), 1)
            pool.wait_ge(s("x_moved"), 32)
            pool_square(pool, SETUP, 0, 0)
            pool_square(pool, SETUP, 0, 2)
            heads(pool, pool_head)

        @block.scalar
        def _(act):
            act.dma_start(m.c_rows[0:KD, :], in_c[0].rearrange("(k p) -> k p", p=P)).then_inc(s("c_loaded"), 16)
            act.dma_start(m.c_rows[KD:2 * KD, :], in_c_ctx.rearrange("(k p) -> k p", p=P)).then_inc(s("c_loaded"), 16)
            act.dma_start(m.const[:, :], in_const).then_inc(s("const"), 16)
            act.dma_start(m.x[0:HALF, :, :], in_x[0].rearrange("(t p) d -> p t d", p=HALF)).then_inc(s("x_loaded"), 16)
            act.dma_start(m.x[HALF:P, :, :], in_ctx[0].rearrange("(t p) d -> p t d", p=HALF)).then_inc(s("x_loaded"), 16)
            act.dma_start(v.pool_scale, in_pool_scale[0].partition_broadcast(P)).then_inc(s("pool_scale"), 16)
            act.dma_start(v.pool_m, in_pool_m.rearrange("p w (t n) -> p w t n", t=MT)).then_inc(s("pool_m"), 16)
            act.dma_start(v.pool_w, in_pool_w[0].rearrange("w (c p) d -> p w c d", p=P)).then_inc(s("pool_w"), 16)
            ln_loads(act, 0, 0)
            act.dma_start(v.w_router, in_w_router.rearrange("(k p) e -> p k e", p=P)).then_inc(s("small_loads"), 16)
            act.dma_start(v.b_router, in_b_router.partition_broadcast(P)).then_inc(s("small_loads"), 16)
            act.wait_ge(s("c_loaded"), 32)
            act.activation(m.c_silu[:, :], m.c_rows[:, :], ACT.Silu).then_inc(s("c_silu"), 1)
            act_mod(act, 0, 0)
            act_mod(act, 1, 0)
            act_pool(act)
            for t in range(MT):
                act_norm(act, "ln0a_", t, t)
            with act.Fori(2, 4) as i:
                act_mod(act, i, 0)
            act.wait_ge(s("ln_x"), MT)
            ln_loads(act, 0, 1)
            act_router(act, L0)
            act_moe(act, L0)
            act_mod(act, 4, 1)
            for t in range(MT):
                act_norm(act, "ln0b_", t, t)
            act_mod(act, 5, 1)
            act.wait_ge(s("ln_x"), 2 * MT)
            ln_loads(act, 1, 0)
            act_dn_small(act)
            act_dn_setup(act)
            act_mod(act, 6, 1)
            act_dn_exps(act)
            act_mod(act, 7, 1)
            act.wait_ge(s("pads"), 3)
            act_dn_first(act)
            heads(act, act_head)
            for t in range(XT):
                act_norm(act, "ln1a_", t, L1.x_tiles[t])
            act.wait_ge(s("ln_x"), 2 * MT + XT)
            ln_loads(act, 1, 1)
            act_router(act, L1)
            act_moe(act, L1)
            for t in range(XT):
                act_norm(act, "ln1b_", t, L1.x_tiles[t])

        @block.tensor
        def _(pe):
            pe.wait_ge(s("c_silu"), 1)
            pe.wait_ge(s("const"), 16)
            pe.transpose(m.ps[:, 7, 0:2 * KD], m.c_silu[:, :], v.ident[0:2 * KD, 0:2 * KD]).then_inc(s("c_turned"), 1)
            pe.wait_ge(s("c_spread"), 3)
            both = lambda i, j: v.c_mix
            pe_mod(pe, 0, both, True)
            pe_mod(pe, 1, both, False)
            pe_pool(pe)
            with pe.Fori(2, 4) as i:
                pe_mod(pe, i, both, False)
            pe_router(pe, L0)
            pe.wait_ge(s("mod_copied"), NCH)
            pe_moe(pe, L0)
            nt, tb = group_counts(pe, N_GROUPS - 1)
            pe.wait_ge(s(L0.tag + "summed"), 4 * tb + 4 * nt + 1)
            of_layer1 = lambda i, j: v.c_mix if 3 * (i - 4) + j < 4 else v.c_lat
            for i in (4, 5):
                pe_mod(pe, i, of_layer1, False)
            pe_dn_setup(pe)
            pe_mod(pe, 6, of_layer1, False)
            pe_dn_cumulate(pe)
            pe_mod(pe, 7, of_layer1, False)
            pe_dn_first(pe)
            heads(pe, pe_head)
            pe_dn_out(pe)
            pe_router(pe, L1)
            pe_moe(pe, L1)

        @block.vector
        def _(dve):
            dve.wait_ge(s("c_turned"), 1)
            cT = m.ps[:, 7, 0:2 * KD]
            lat = cT[:, 0:KD].unsqueeze(2).to_broadcast([P, KD, HALF])
            ctx_c = cT[:, KD:2 * KD].unsqueeze(2).to_broadcast([P, KD, HALF])
            dve.tensor_copy(v.c_mix[:, :, 0:HALF], lat).then_inc(s("c_spread"), 1)
            dve.tensor_copy(v.c_mix[:, :, HALF:P], ctx_c).then_inc(s("c_spread"), 1)
            dve.tensor_copy(v.c_lat, cT[:, 0:KD].unsqueeze(2).to_broadcast([P, KD, P])).then_inc(s("c_spread"), 1)

            def first_h(tag, biased):
                dve.wait_ge(s("mod_biased"), biased)
                for t in range(MT):
                    h = m.h[:, t, :]
                    dve.scalar_tensor_tensor(out=h, in0=mod_vec(SCALE1), scalar=1.0, in1=m.x[:, t, :],
                                             op0=ALU.add, op1=ALU.mult).then_inc(s(tag + "scaled"), 1)
                    dve.wait_ge(s(tag + "scaled"), t + 1)
                    dve.tensor_tensor(h, h, mod_vec(SHIFT1), ALU.add).then_inc(s(tag + "h"), 1)

            dve.wait_ge(s("x_loaded"), 32)
            first_h("in0_", 4)
            dve.wait_ge(s("mod_biased"), 6)
            dve.wait_ge(s("pool_scale"), 16)
            dve.tensor_tensor(mod_vec(GATE1), mod_vec(GATE1), v.pool_scale, ALU.mult).then_inc(s("pool_gate"), 1)
            dve.wait_ge(s("pool_gate"), 1)
            dve.wait_ge(s("const"), 16)
            for t in range(MT):
                dve_norm(dve, "ln0a_", t, t, pool_y, lambda n: dve.wait_ge(s("pool_y"), n + 1), mod_vec(GATE1),
                         None, lambda: dve.wait_ge(s("ln_vec"), 32))
            dve.wait_ge(s("mod_biased"), 10)
            for t in range(MT):
                dve_modulate(dve, "ln0a_", t, t, t, (SHIFT2, SCALE2))
            dve_router(dve, L0)
            dve_moe(dve, L0)
            dve.wait_ge(s("mod_biased"), NCH)
            dve.wait_ge(s("moe0_y_added"), 2)
            for t in range(MT):
                dve_norm(dve, "ln0b_", t, t, lambda n: v.y_rows[:, n, :], lambda n: None, mod_vec(GATE2),
                         None, lambda: dve.wait_ge(s("ln_vec"), 64))
            dve.wait_ge(s("ln_x"), 2 * MT)
            first_h("in1_", NCH + 4)
            dve_dn_setup(dve)
            heads(dve, dve_head)
            dve.wait_ge(s("mod_biased"), 2 * NCH)
            dve.wait_ge(s("x_moved"), 32)
            for t in range(XT):
                dve_norm(dve, "ln1a_", t, L1.x_tiles[t], dn_y, lambda n: dve.wait_ge(s("dn_y"), n + 1), mod_vec(GATE1),
                         None, lambda: dve.wait_ge(s("ln_vec"), 96))
            dve.wait_ge(s("dn_y"), XT)
            for t in range(XT):
                dve_modulate(dve, "ln1a_", t, L1.x_tiles[t], t, (SHIFT2, SCALE2))
            dve_router(dve, L1)
            dve_moe(dve, L1)
            dve.wait_ge(s("moe1_y_added"), 2)
            for t in range(XT):
                dve_norm(dve, "ln1b_", t, L1.x_tiles[t], lambda n: v.y_rows[:, n, :], lambda n: None, mod_vec(GATE2),
                         None, lambda: dve.wait_ge(s("ln_vec"), 128))


def constants():
    import numpy as np
    i, j = np.arange(P)[:, None], np.arange(P)[None, :]
    c = np.zeros((P, N_CONST * P), np.float32)

    def put(at, value):
        c[:, at * P:at * P + value.shape[1]] = value
    put(C_IDENT, i == j)
    put(C_ONES, np.ones((P, P)))
    put(C_UPPER, i < j)
    put(C_UPPER_IN, i <= j)
    put(C_LOWER_IN, i >= j)
    put(C_IOTA, np.tile(np.arange(1, MT * P + 1), (P, 1)))
    put(C_NEG_F, np.where(i <= j, 0.0, -1e30))
    put(C_NEG_B, np.where(i >= j, 0.0, -1e30))
    for n in range(LEVELS):
        b = 2 ** n
        joined = (i // (2 * b) == j // (2 * b)) & (i // b != j // b)
        put(C_LEVEL_F + n, joined & (i > j))
        put(C_LEVEL_B + n, joined & (i < j))

    def box(n, k):
        b = np.zeros((n, n))
        for t in range(n):
            lo, hi = max(t - k // 2, 0), min(t + k - k // 2, n)
            b[t, lo:hi] = 1.0 / (hi - lo)
        return b
    pool = np.zeros((NW, MT * P, MT * P), np.float32)
    n = np.arange(MT * P)
    lat = (n % P) < HALF
    place = (n // P) * HALF + n % HALF
    for w, k in enumerate(WINDOWS):
        grid = np.kron(box(SEQ // GRID_W, k), box(GRID_W, k))
        line = box(CTX, k)
        full = np.zeros((MT * P, MT * P))
        full[np.ix_(lat, lat)] = grid[np.ix_(place[lat], place[lat])]
        full[np.ix_(~lat, ~lat)] = line[np.ix_(place[~lat], place[~lat])]
        pool[w] = (full - np.eye(MT * P)).T
    pool = pool.reshape(NW, MT, P, MT * P).transpose(2, 0, 1, 3).reshape(P, NW, MT * MT * P)
    return c, np.ascontiguousarray(pool)


_INS = ["x", "c", "ctx", "c_ctx", "w_mod", "b_mod", "ln_g", "ln_b", "pool_w", "pool_scale", "dn_w_in", "dn_conv",
        "dn_a_log", "dn_dt_bias", "dn_norm", "dn_w_out", "w_router", "b_router", "w_gate", "w_up", "w_down"]


def kernel(**inputs):
    import numpy as _np
    import concourse.bacc as _bacc
    from concourse.bass_utils import run_bass_kernel_spmd as _run

    nc = _bacc.Bacc("TRN2", target_bir_lowering=False, num_devices=1)
    const, pool_m = constants()
    given = [(name, inputs[name]) for name in _INS] + [("const", const), ("pool_m", pool_m)]
    arrays, args = {}, []
    for name, a in given:
        a = _np.ascontiguousarray(a)
        arrays[f"in_{name}_dram"] = a
        args.append(nc.dram_tensor(f"in_{name}_dram", a.shape, F32, kind="ExternalInput").ap())
    args.append(nc.dram_tensor("out_dram", (1, SEQ, D), F32, kind="ExternalOutput").ap())
    build(nc, *args)
    return _run(nc, [arrays], core_ids=[0]).results[0]["out_dram"]
```
